# Optimizing a Trainium2 kernel written in Bass

```python
import jax, jax.numpy as jnp
from jax import lax
import numpy as np

D_MODEL = 1024
BATCH = 1
SEQ = 256
DEPTH = 1
DEC_BATCH = 8
DEC_SEQ = 4
PAST_LEN = 256
PAGE_SIZE = 128

HEAD_DIM = 64
GROUP_WIDTH = D_MODEL // 2
GROUP_HEADS = GROUP_WIDTH // HEAD_DIM
N_KV_HEADS = 2 * GROUP_HEADS
MOBA_BLOCK = 256
MOBA_TOP_K = 3
Q_BLOCK = 128
ROPE_THETA = 10000.0
N_MEM = 256
MEM_HEADS = 4
MEM_HEAD_DIM = D_MODEL // MEM_HEADS
MEM_WIDTH = MEM_HEADS * MEM_HEAD_DIM
N_EXPERTS = 32
TOP_K = 4
D_FF = D_MODEL
SWIGLU_LIMIT = 7.0
SWIGLU_ALPHA = 1.702
EXPERT_BLOCK = 128
DEEPNORM_ALPHA = (2 * DEPTH) ** 0.25
DEEPNORM_BETA = (8 * DEPTH) ** -0.25
LN_EPS = 1e-5
RMS_EPS = 1e-6
ATT_SCALE = HEAD_DIM ** -0.5
F32 = jnp.float32

kernel_name = 'moba_stickbreak_hybrid_decode_step'

def layer_norm(x, g, b):
    xf = x.astype(F32)
    xc = xf - jnp.mean(xf, axis=-1, keepdims=True)
    var = jnp.mean(xc * xc, axis=-1, keepdims=True)
    return (xc * lax.rsqrt(var + LN_EPS) * g + b).astype(x.dtype)

def rms_norm(x, g):
    xf = x.astype(F32)
    return (xf * lax.rsqrt(jnp.mean(xf * xf, axis=-1, keepdims=True) + RMS_EPS) * g).astype(x.dtype)

def rope(x, pos):
    half = HEAD_DIM // 2
    inv_freq = ROPE_THETA ** (-jnp.arange(half, dtype=F32) / half)
    ang = pos.astype(F32)[:, None] * inv_freq[None, :]
    cos = jnp.cos(ang)[None, :, None, :]
    sin = jnp.sin(ang)[None, :, None, :]
    xf = x.astype(F32)
    x1, x2 = xf[..., :half], xf[..., half:]
    return jnp.concatenate([x1 * cos - x2 * sin, x2 * cos + x1 * sin], axis=-1).astype(x.dtype)

def project_groups(x, pos, w_in):
    b, t, _ = x.shape
    parts = jnp.split(x @ w_in, 6, axis=-1)
    qa, ka, va, qb, kb, vb = [p.reshape(b, t, GROUP_HEADS, HEAD_DIM) for p in parts]
    return rope(qa, pos), rope(ka, pos), va, qb, kb, vb

def merge_groups(oa, ob, g_moba, g_sb, w_out):
    b, t = oa.shape[:2]
    y = jnp.concatenate([rms_norm(oa.reshape(b, t, GROUP_WIDTH), g_moba),
                         rms_norm(ob.reshape(b, t, GROUP_WIDTH), g_sb)], axis=-1)
    return y @ w_out

def to_blocks(k, v):
    b, l, h, hd = k.shape
    nb = -(-l // MOBA_BLOCK)
    pad = nb * MOBA_BLOCK - l
    def blk(t):
        return jnp.pad(t, ((0, 0), (0, pad), (0, 0), (0, 0))).reshape(b, nb, MOBA_BLOCK, h, hd).transpose(0, 3, 1, 2, 4)
    kb, vb = blk(k), blk(v)
    kbar = jnp.mean(kb.astype(F32), axis=3)
    return kb, vb, kbar

def moba_core(q, q_pos, kb, vb, kbar):
    h, nb = kb.shape[0], kb.shape[1]
    nq = q.shape[0]
    n_sel = min(MOBA_TOP_K, nb)
    own = q_pos // MOBA_BLOCK
    gate = jnp.einsum('qhd,hnd->qhn', q.astype(F32), kbar)
    gate = jnp.where(jnp.arange(nb)[None, None, :] < own[:, None, None], gate, -jnp.inf)
    _, sel = lax.top_k(gate, n_sel)
    sel_ok = sel < own[:, None, None]
    h_idx = jnp.arange(h)[None, :, None]
    k_sel = kb[h_idx, sel]
    v_sel = vb[h_idx, sel]
    k_own = kb[:, own]
    v_own = vb[:, own]
    s_sel = jnp.einsum('qhd,qhnkd->qhnk', q, k_sel, preferred_element_type=F32) * ATT_SCALE
    s_sel = jnp.where(sel_ok[..., None], s_sel, -jnp.inf).reshape(nq, h, n_sel * MOBA_BLOCK)
    s_own = jnp.einsum('qhd,hqkd->qhk', q, k_own, preferred_element_type=F32) * ATT_SCALE
    key_pos = own[:, None] * MOBA_BLOCK + jnp.arange(MOBA_BLOCK)[None, :]
    s_own = jnp.where((key_pos <= q_pos[:, None])[:, None, :], s_own, -jnp.inf)
    p = jax.nn.softmax(jnp.concatenate([s_sel, s_own], axis=-1), axis=-1).astype(vb.dtype)
    p_sel = p[..., :n_sel * MOBA_BLOCK].reshape(nq, h, n_sel, MOBA_BLOCK)
    p_own = p[..., n_sel * MOBA_BLOCK:]
    return jnp.einsum('qhnk,qhnkd->qhd', p_sel, v_sel) + jnp.einsum('qhk,hqkd->qhd', p_own, v_own)

def moba_prompt(q, k, v):
    b, s, h, hd = q.shape
    nc = s // Q_BLOCK
    kb, vb, kbar = to_blocks(k, v)
    qc = q.reshape(b * nc, Q_BLOCK, h, hd)
    b_idx = jnp.repeat(jnp.arange(b), nc)
    pos = jnp.tile(jnp.arange(s).reshape(nc, Q_BLOCK), (b, 1))
    def step(a):
        qi, bi, pi = a
        return moba_core(qi, pi, kb[bi], vb[bi], kbar[bi])
    return lax.map(step, (qc, b_idx, pos)).reshape(b, s, h, hd)

def stick_breaking(q, q_pos, k, v):
    l = k.shape[1]
    z = jnp.einsum('bqhd,bkhd->bhqk', q, k, preferred_element_type=F32) * ATT_SCALE
    strict = jnp.arange(l)[None, :] < q_pos[:, None]
    log_keep = jnp.where(strict, jax.nn.log_sigmoid(-z), 0.0)
    after = lax.cumsum(log_keep, axis=3, reverse=True) - log_keep
    a = jnp.where(strict, jnp.exp(jax.nn.log_sigmoid(z) + after), 0.0)
    return jnp.einsum('bhqk,bkhd->bqhd', a.astype(v.dtype), v)

def sb_prompt(q, k, v):
    b, s, h, hd = q.shape
    nc = s // Q_BLOCK
    qc = q.reshape(b, nc, Q_BLOCK, h, hd).transpose(1, 0, 2, 3, 4)
    pos = jnp.arange(s).reshape(nc, Q_BLOCK)
    out = lax.map(lambda a: stick_breaking(a[0], a[1], k, v), (qc, pos))
    return out.transpose(1, 0, 2, 3, 4).reshape(b, s, h, hd)

def gather_past(cache, layer, page_table, h0, h1):
    rows = cache[layer, page_table, :, h0:h1]
    return rows.reshape(page_table.shape[0], page_table.shape[1] * PAGE_SIZE, h1 - h0, HEAD_DIM)

def mem_kv(mem, w_mkv):
    b, m, _ = mem.shape
    mk, mv = jnp.split(mem @ w_mkv, 2, axis=-1)
    return mk.reshape(b, m, MEM_HEADS, MEM_HEAD_DIM), mv.reshape(b, m, MEM_HEADS, MEM_HEAD_DIM)

def mem_attend(x, mk, mv, w_mq, w_mo):
    b, t, _ = x.shape
    q = (x @ w_mq).reshape(b, t, MEM_HEADS, MEM_HEAD_DIM)
    s = jnp.einsum('bthd,bmhd->bhtm', q, mk, preferred_element_type=F32) * MEM_HEAD_DIM ** -0.5
    p = jax.nn.softmax(s, axis=-1).astype(mv.dtype)
    o = jnp.einsum('bhtm,bmhd->bthd', p, mv).reshape(b, t, MEM_WIDTH)
    return o @ w_mo

def moe_ffn(h, w_router, b_router, w_gu, b_gu, w_down, b_down):
    t, d = h.shape
    logits = jnp.matmul(h, w_router, preferred_element_type=F32) + b_router
    top_val, top_e = lax.top_k(logits, TOP_K)
    gates = jax.nn.softmax(top_val, axis=-1)
    n_assign = t * TOP_K
    flat_e = top_e.reshape(n_assign)
    order = jnp.argsort(flat_e)
    e_sorted = flat_e[order]
    tok_sorted = (order // TOP_K).astype(jnp.int32)
    gate_sorted = gates.reshape(n_assign)[order]
    counts = jnp.bincount(flat_e, length=N_EXPERTS)
    padded = (counts + EXPERT_BLOCK - 1) // EXPERT_BLOCK * EXPERT_BLOCK
    pad_end = jnp.cumsum(padded)
    pad_start = pad_end - padded
    start = jnp.cumsum(counts) - counts
    dest = pad_start[e_sorted] + jnp.arange(n_assign) - start[e_sorted]
    n_blocks = -(-(n_assign + N_EXPERTS * (EXPERT_BLOCK - 1)) // EXPERT_BLOCK)
    n_rows = n_blocks * EXPERT_BLOCK
    row_tok = jnp.full((n_rows,), t, jnp.int32).at[dest].set(tok_sorted)
    row_gate = jnp.zeros((n_rows,), F32).at[dest].set(gate_sorted)
    block_e = jnp.minimum(jnp.searchsorted(pad_end, jnp.arange(n_blocks) * EXPERT_BLOCK, side='right'), N_EXPERTS - 1)
    h_pad = jnp.concatenate([h, jnp.zeros((1, d), h.dtype)], axis=0)
    xb = h_pad[row_tok].reshape(n_blocks, EXPERT_BLOCK, d)
    def expert_block(a):
        xi, e = a
        gate, up = jnp.split(xi @ w_gu[e] + b_gu[e], 2, axis=-1)
        gate = jnp.minimum(gate, SWIGLU_LIMIT)
        up = jnp.clip(up, -SWIGLU_LIMIT, SWIGLU_LIMIT)
        act = (up + 1.0) * gate * jax.nn.sigmoid(SWIGLU_ALPHA * gate)
        return act @ w_down[e] + b_down[e]
    yb = lax.map(expert_block, (xb, block_e)).reshape(n_rows, d)
    out = jnp.zeros((t + 1, d), F32).at[row_tok].add(yb.astype(F32) * row_gate[:, None])
    return out[:t].astype(h.dtype)

def setup_inputs(seed: int = 0) -> dict:
    key = jax.random.key(seed)
    ks = jax.random.split(key, 32)
    def nrm(i, shape, scale):
        return jax.random.normal(ks[i], shape, F32) * scale
    n_pages = PAST_LEN // PAGE_SIZE
    n_used = DEC_BATCH * n_pages
    n_phys = n_used + max(1, n_used // 4)
    page_table = jax.random.permutation(ks[0], n_phys)[:n_used].reshape(DEC_BATCH, n_pages).astype(jnp.int32)
    L, D, GW, E, F = DEPTH, D_MODEL, GROUP_WIDTH, N_EXPERTS, D_FF
    return {
        'x_prompt': nrm(1, (BATCH, SEQ, D), 1.0),
        'x_sample': nrm(2, (DEC_BATCH, DEC_SEQ, D), 1.0),
        'mem_prompt': nrm(3, (BATCH, N_MEM, D), 1.0),
        'cache_k': nrm(4, (L, n_phys, PAGE_SIZE, N_KV_HEADS, HEAD_DIM), 1.0),
        'cache_v': nrm(5, (L, n_phys, PAGE_SIZE, N_KV_HEADS, HEAD_DIM), 1.0),
        'cache_mem_k': nrm(6, (L, DEC_BATCH, N_MEM, MEM_HEADS, MEM_HEAD_DIM), 1.0),
        'cache_mem_v': nrm(7, (L, DEC_BATCH, N_MEM, MEM_HEADS, MEM_HEAD_DIM), 1.0),
        'page_table': page_table,
        'w_in': nrm(8, (L, D, 6 * GW), D ** -0.5),
        'g_moba': 1.0 + nrm(9, (L, GW), 0.02),
        'g_sb': 1.0 + nrm(10, (L, GW), 0.02),
        'w_out': nrm(11, (L, 2 * GW, D), (2 * GW) ** -0.5 * DEEPNORM_BETA),
        'ln1_g': 1.0 + nrm(12, (L, D), 0.02),
        'ln1_b': nrm(13, (L, D), 0.02),
        'w_mq': nrm(14, (L, D, MEM_WIDTH), D ** -0.5),
        'w_mkv': nrm(15, (L, D, 2 * MEM_WIDTH), D ** -0.5),
        'w_mo': nrm(16, (L, MEM_WIDTH, D), MEM_WIDTH ** -0.5 * DEEPNORM_BETA),
        'ln2_g': 1.0 + nrm(17, (L, D), 0.02),
        'ln2_b': nrm(18, (L, D), 0.02),
        'w_router': nrm(19, (L, D, E), D ** -0.5),
        'b_router': nrm(20, (L, E), 0.01),
        'w_gu': nrm(21, (L, E, D, 2 * F), D ** -0.5),
        'b_gu': nrm(22, (L, E, 2 * F), 0.02),
        'w_down': nrm(23, (L, E, F, D), F ** -0.5 * DEEPNORM_BETA),
        'b_down': nrm(24, (L, E, D), 0.02),
        'ln3_g': 1.0 + nrm(25, (L, D), 0.02),
        'ln3_b': nrm(26, (L, D), 0.02),
    }

def reference(x_prompt, x_sample, mem_prompt, cache_k, cache_v, cache_mem_k, cache_mem_v, page_table,
              w_in, g_moba, g_sb, w_out, ln1_g, ln1_b,
              w_mq, w_mkv, w_mo, ln2_g, ln2_b,
              w_router, b_router, w_gu, b_gu, w_down, b_down, ln3_g, ln3_b):
    n_seq, seq_len, d = x_prompt.shape
    n_dec, dec_len, _ = x_sample.shape
    past_len = page_table.shape[1] * PAGE_SIZE
    pos_p = jnp.arange(seq_len)
    pos_s = past_len + jnp.arange(dec_len)
    n_tok_p = n_seq * seq_len
    xp, xs = x_prompt, x_sample
    new_kp, new_vp, new_ks, new_vs, mem_kp, mem_vp = [], [], [], [], [], []
    for l in range(DEPTH):
        qa, ka, va, qb, kb, vb = project_groups(xp, pos_p, w_in[l])
        mix_p = merge_groups(moba_prompt(qa, ka, va), sb_prompt(qb, kb, vb), g_moba[l], g_sb[l], w_out[l])
        new_kp.append(jnp.concatenate([ka, kb], axis=2))
        new_vp.append(jnp.concatenate([va, vb], axis=2))
        qa_s, ka_s, va_s, qb_s, kb_s, vb_s = project_groups(xs, pos_s, w_in[l])
        ka_all = jnp.concatenate([gather_past(cache_k, l, page_table, 0, GROUP_HEADS), ka_s], axis=1)
        va_all = jnp.concatenate([gather_past(cache_v, l, page_table, 0, GROUP_HEADS), va_s], axis=1)
        kb_all = jnp.concatenate([gather_past(cache_k, l, page_table, GROUP_HEADS, N_KV_HEADS), kb_s], axis=1)
        vb_all = jnp.concatenate([gather_past(cache_v, l, page_table, GROUP_HEADS, N_KV_HEADS), vb_s], axis=1)
        kblk, vblk, kbar = to_blocks(ka_all, va_all)
        oa_s = lax.map(lambda a: moba_core(a[0], pos_s, a[1], a[2], a[3]), (qa_s, kblk, vblk, kbar))
        ob_s = stick_breaking(qb_s, pos_s, kb_all, vb_all)
        mix_s = merge_groups(oa_s, ob_s, g_moba[l], g_sb[l], w_out[l])
        new_ks.append(jnp.concatenate([ka_s, kb_s], axis=2))
        new_vs.append(jnp.concatenate([va_s, vb_s], axis=2))
        xp = layer_norm(DEEPNORM_ALPHA * xp + mix_p, ln1_g[l], ln1_b[l])
        xs = layer_norm(DEEPNORM_ALPHA * xs + mix_s, ln1_g[l], ln1_b[l])
        mk, mv = mem_kv(mem_prompt, w_mkv[l])
        mem_kp.append(mk)
        mem_vp.append(mv)
        xp = layer_norm(DEEPNORM_ALPHA * xp + mem_attend(xp, mk, mv, w_mq[l], w_mo[l]), ln2_g[l], ln2_b[l])
        xs = layer_norm(DEEPNORM_ALPHA * xs + mem_attend(xs, cache_mem_k[l], cache_mem_v[l], w_mq[l], w_mo[l]), ln2_g[l], ln2_b[l])
        tok = jnp.concatenate([xp.reshape(n_tok_p, d), xs.reshape(n_dec * dec_len, d)], axis=0)
        ffn = moe_ffn(tok, w_router[l], b_router[l], w_gu[l], b_gu[l], w_down[l], b_down[l])
        tok = layer_norm(DEEPNORM_ALPHA * tok + ffn, ln3_g[l], ln3_b[l])
        xp = tok[:n_tok_p].reshape(n_seq, seq_len, d)
        xs = tok[n_tok_p:].reshape(n_dec, dec_len, d)
    return (xp, xs, jnp.stack(new_kp), jnp.stack(new_vp), jnp.stack(new_ks), jnp.stack(new_vs), jnp.stack(mem_kp), jnp.stack(mem_vp))


_drawn_inputs = setup_inputs


def setup_inputs(seed=0):
    import zlib

    import numpy as np

    out = dict(_drawn_inputs(seed))
    spreads = {}
    factors = {'g_moba': 8.354,
     'g_sb': 3.744,
     'b_gu': 8.0,
     'b_down': 6.235,
     'ln3_g': 7.882,
     'ln3_b': 7.864,
     'b_router': 3.424}
    for name, (base, spread) in spreads.items():
        noise = np.random.default_rng([zlib.crc32(name.encode()), seed]).standard_normal(out[name].shape)
        drawn = base * np.exp(spread * noise) if base else spread * noise
        out[name] = __import__('jax').numpy.asarray(drawn.astype(out[name].dtype))
    for name, factor in factors.items():
        out[name] = (out[name] * factor).astype(out[name].dtype)
    return out
```

```python
from contextlib import ExitStack

import concourse.bass as bass
from concourse import mybir

F32 = mybir.dt.float32
BF16 = mybir.dt.bfloat16
I32 = mybir.dt.int32
U32 = mybir.dt.uint32
ALU = mybir.AluOpType
ACT = mybir.ActivationFunctionType
AX = mybir.AxisListType.X

P = 128
D = 1024
KB = D // P
NPT = 256
NB_DEC, Q_DEC = 8, 4
NS = NB_DEC * Q_DEC
T = NPT + NS
CHUNKS = ((0, 128), (128, 128), (256, NS))
PAST = 256
PAGES = 2
N_PHYS = 20
HD = 64
NPAIR = 8
ATT_SCALE = HD ** -0.5
MEM_H = 4
MEM_SCALE = 256.0 ** -0.5
N_MEM = 256
ALPHA = 2.0 ** 0.25
LN_EPS, RMS_EPS = 1e-5, 1e-6
NE = 32
TOPK = 4
CAP = 64
LIMIT, SW_ALPHA = 7.0, 1.702
NEG = -1.0e30

RING = 12
SLOT = 2048
EARLY = 6
ROT = 4

CONST = {}
_at = 0
for _name, _n in (("ident", 128), ("rot", 128), ("cos", T), ("sin", T), ("causal", 128), ("strict", 128),
                  ("strict_add", 128), ("new_causal", 64), ("new_strict", 64), ("new_strict_add", 64),
                  ("tri", 128), ("one", 128), ("one1024", 128), ("one512", 128), ("slot2", 128), ("iota", 320), ("eye3", 32),
                  ("zero", 1)):
    CONST[_name] = (_at, _n)
    _at += _n
CONST_W = _at


def const_table():
    import numpy as np

    c = np.zeros((P, CONST_W), np.float32)

    def put(name, a):
        at, n = CONST[name]
        c[: a.shape[0], at:at + n] = a

    r = np.arange(P)
    put("ident", np.eye(P))
    rot = np.zeros((P, P))
    for m in range(P):
        if m % 64 < 32:
            rot[m + 32, m] = -1.0
        else:
            rot[m - 32, m] = 1.0
    put("rot", rot)
    half = HD // 2
    inv = (np.float32(10000.0) ** (-np.arange(half, dtype=np.float32) / np.float32(half))).astype(np.float32)
    pos = np.concatenate([np.arange(NPT), PAST + np.arange(NS) % Q_DEC]).astype(np.float32)
    ang = (pos[None, :] * inv[r % half][:, None]).astype(np.float32)
    put("cos", np.cos(ang.astype(np.float64)))
    put("sin", np.sin(ang.astype(np.float64)))
    put("causal", np.where(r[None, :] <= r[:, None], 0.0, NEG))
    put("strict", (r[None, :] < r[:, None]) * 1.0)
    put("strict_add", np.where(r[None, :] < r[:, None], 0.0, NEG))
    for quad in range(2):
        j = np.arange(NS)
        q = r % 4
        for name, g in (("new_causal", 0), ("new_strict", 1), ("new_strict_add", 1)):
            b = 4 * quad + (r // 32 - 2 * g) % 4
            same = (j[None, :] // 4) == b[:, None]
            ok = same & ((j[None, :] % 4 <= q[:, None]) if g == 0 else (j[None, :] % 4 < q[:, None]))
            at = CONST[name][0] + quad * NS
            c[:, at:at + NS] = ok if name == "new_strict" else np.where(ok, 0.0, NEG)
    put("tri", (r[:, None] < r[None, :]) * 1.0)
    put("one", np.ones((P, P)))
    put("one1024", np.full((P, P), 1 / 1024))
    put("one512", np.full((P, P), 1 / 512))
    put("slot2", np.tile(np.arange(CAP), 2)[None, :].repeat(P, 0))
    put("eye3", np.tile(np.eye(32), (3, 1)))
    put("iota", np.arange(320)[None, :].repeat(P, 0))
    return c


def plan_items():
    items = [("xp",), ("xs",)]
    items += [("w", "k", i) for i in range(4)] + [("w", "q", i) for i in range(4)] + [("w", "v", i) for i in range(4)]
    items += [("mem",)] + [("w", "mv", i) for i in range(4)]
    items += [("ck", b) for b in range(6)] + [("cv", b) for b in range(4)]
    items += [("ck", 6), ("ck", 7)] + [("cv", b) for b in range(4, 8)]
    items += [("w", "o", i) for i in range(4)] + [("w", "mk", i) for i in range(4)]
    items += [("w", "mq", i) for i in range(4)]
    items += [("mk", b) for b in range(8)] + [("mv", b) for b in range(8)]
    items += [("w", "mo", i) for i in range(4)]
    return items


ITEMS = plan_items()
PAIR_ORDER = [0, 4, 1, 5, 2, 6, 3, 7]


def build(nc, A, O):
    ctx = ExitStack()
    with ctx:
        def sb(name, shape, dt=F32):
            return ctx.enter_context(nc.sbuf_tensor(name, shape, dt))

        def sem(name):
            return ctx.enter_context(nc.semaphore(name))

        ring = sb("ring", [P, RING * SLOT])
        consts = sb("consts", [P, CONST_W])
        area = sb("area", [P, 25000])
        pages = sb("pages", [1, NB_DEC * PAGES], I32)
        vec_rows = sb("vec_rows", [40, P])
        vec = sb("vec", [P, 40])
        small = sb("small", [P, 32])
        eps_small = sb("eps_small", [P, 2])
        bank = [ctx.enter_context(nc.psum_tensor(f"bank{i}", [P, 512], F32)) for i in range(8)]

        def C(name, a=0, b=None, rows=P):
            at, n = CONST[name]
            return consts[0:rows, at + a:at + (n if b is None else b)]

        def carve(base, at, *shape):
            n = 1
            for s in shape:
                n *= s
            v = base[:, at:at + n]
            if len(shape) == 2:
                v = v.rearrange("p (a b) -> p a b", a=shape[0])
            elif len(shape) == 3:
                v = v.rearrange("p (a b c) -> p a b c", a=shape[0], b=shape[1])
            return v

        def slot(i):
            return ring[:, i * SLOT:(i + 1) * SLOT]

        W0 = EARLY * SLOT
        xT = carve(ring, W0, KB, T)
        x2T = xT
        kT = carve(ring, W0 + 2304, NPAIR, T)
        x1T = kT
        mqT = carve(ring, W0 + 4608, KB, T)
        raw = carve(ring, W0 + 4608, 2, T)
        qf = carve(ring, W0 + 4608 + 576, 2, T)
        rope_t = carve(ring, W0 + 4608 + 1152, 2, T)
        aT = carve(ring, W0 + 6912, KB, T)
        oT = aT
        V = carve(ring, W0 + 9216, 3, D)
        yT = carve(ring, W0 + 9216, KB, T)

        ktb = [carve(area, i * 2304, NPAIR, T) for i in range(2)]
        sqT = carve(area, 0, KB, T)
        qx = carve(area, 4608, NB_DEC * NPAIR, 32)
        memT = carve(area, 6656, KB, N_MEM)
        mkT = carve(area, 8704, KB, N_MEM)
        mvN = carve(area, 10752, 2, D)
        knat = carve(area, 6656, 3, D)
        qz = carve(area, 12800, NPAIR * 2, NPT)
        mknat = carve(area, 12800, 2, D)
        tmp = [carve(area, 16896 + 768 * i, 768) for i in range(8)]
        so = [carve(area, 14848 + 512 * g, 512) for g in range(2)]
        lnv = area[:, 16212:16212 + T]
        rstd = area[:, 16500:16500 + T]
        ptb = [[carve(area, 23040 + 384 * (2 * i + hh), 384) for hh in range(2)] for i in range(2)]
        ptq = [carve(area, 23040 + 384 * g, 3, P) for g in range(2)]

        tokn = area[:, 0:4608].bitcast(BF16).rearrange("p (s c n) -> p s c n", s=3, c=3)
        acc = carve(area, 4608, 3, D)
        acc2 = area[0:64, 7680:8192]
        xgT = carve(area, 8192, KB, CAP)
        gate_s = carve(area, 8704, 512)
        sig_s = carve(area, 9216, 512)
        up_s = carve(area, 9728, 512)
        act_s = carve(area, 10240, 512)
        actT = carve(area, 10752, 4, P)
        y_s = carve(area, 11264, 512)
        selT = [carve(area, 11776 + 288 * i, T) for i in range(2)]
        pick = area[:, 12352:12352 + 96].bitcast(BF16).rearrange("p (c n) -> p c n", c=3)
        gpick = carve(area, 12448, 3, P)
        rankm = carve(area, 12832, 3, NE)
        gates = carve(area, 12928, 3, NE)
        mask = carve(area, 13024, 3, NE)
        rcol = area[:, 13120:13123]
        gcol = area[:, 13124:13127]
        slots_now = area[:, 13128:13128 + 128]
        ebias = area[:, 13256:13256 + 32].bitcast(BF16)
        logT = area[:, 13288:13288 + T]
        logit = carve(area, 13576, 3, NE)
        top = carve(area, 13672, 3, 8)
        topi = area[:, 13696:13720].bitcast(U32).rearrange("p (c n) -> p c n", c=3)
        topf = carve(area, 13720, 3, 8)
        gk = carve(area, 13744, 3, TOPK)
        eq = carve(area, 13760, 3, TOPK, NE)
        eqg = carve(area, 14144, 3, TOPK, NE)
        gT = area[:, 14528:14528 + T]
        nxf = area[:, 14816:14848]
        nxt = area[:, 14848:14880]
        nextra = area[:, 14880:14912].bitcast(I32)
        ebias_src = area[:, 14912:14928].bitcast(BF16)
        bgu = area[0:96, 14928:14928 + 1024].bitcast(BF16)
        w_router = carve(area, 15952, KB, NE)
        b_router = area[0:NE, 16208:16209]
        bdown = area[:, 16896:17920]
        ln3 = carve(area, 17920, 2, D)
        bgu_f = area[0:96, 19968:19968 + 2048]
        bgu_r = area[0:96, 22016:22016 + 2048]
        bgu_b = area[0:96, 24064:24064 + 512].bitcast(BF16)

        const_in = sem("const_in")
        pages_in = sem("pages_in")
        vec_in = sem("vec_in")
        early_in = [sem(f"early_in{i}") for i in range(EARLY)]
        item_used = sem("item_used")
        expert_in = [sem(f"expert_in{i}") for i in range(RING)]
        chunk_used = sem("chunk_used")
        bank_full = [sem(f"bank_full{i}") for i in range(ROT)]
        bank_read = [sem(f"bank_read{i}") for i in range(ROT)]
        dve_step = sem("dve_step")
        act_step = sem("act_step")
        pool_step = sem("pool_step")
        zeroed = sem("zeroed")
        eps_ready = sem("eps_ready")
        roped = sem("roped")
        stick_ready = sem("stick_ready")
        scores_read = [sem(f"scores_read{i}") for i in range(2)]
        out_read = [sem(f"out_read{i}") for i in range(2)]
        s_stick = sem("s_stick")
        centered = sem("centered")
        rms_done = sem("rms_done")
        moe_dve = sem("moe_dve")
        qf_ready = sem("qf_ready")
        qz_done = sem("qz_done")
        qx_done = sem("qx_done")
        new_keys = sem("new_keys")
        kv_stored = sem("kv_stored")
        stored = sem("stored")
        prob_ready = sem("prob_ready")
        max_ready = sem("max_ready")
        exp_ready = sem("exp_ready")
        log_ready = sem("log_ready")
        arg_ready = sem("arg_ready")
        s_scored = sem("s_scored")
        s_prob = sem("s_prob")
        s_pv = sem("s_pv")
        sq_ready = sem("sq_ready")
        rstd_ready = sem("rstd_ready")
        norm_mul = sem("norm_mul")
        norm_done = sem("norm_done")
        late_in = sem("late_in")
        mqx_done = sem("mqx_done")
        tables_in = sem("tables_in")
        router_exp = sem("router_exp")
        router_go = sem("router_go")
        route_ready = sem("route_ready")
        x2_used = sem("x2_used")
        moe_ready = sem("moe_ready")
        sel_ready = sem("sel_ready")
        picked = sem("picked")
        xg_ready = sem("xg_ready")
        gu_done = sem("gu_done")
        sig_in = sem("sig_in")
        sig_ready = sem("sig_ready")
        act_ready = sem("act_ready")
        act_turned = sem("act_turned")
        actT_ready = sem("actT_ready")
        sel_turned = sem("sel_turned")
        selT_ready = sem("selT_ready")
        down_done = sem("down_done")
        y_ready = sem("y_ready")
        comb = sem("comb")
        added = sem("added")
        fin_var = sem("fin_var")
        fin_rstd = sem("fin_rstd")
        fin_ready = sem("fin_ready")

        fills = {}

        def use_of(name):
            return fills[name] % ROT, fills[name] // ROT

        def await_fill(eng, name):
            b, n = use_of(name)
            eng.wait_ge(bank_full[b], n + 1)
            return bank[b]

        def read_sem(name):
            return bank_read[use_of(name)[0]]

        def await_read(eng, name):
            b, n = use_of(name)
            eng.wait_ge(bank_read[b], n + 1)

        def await_query(eng, m):
            if m < 4:
                eng.wait_ge(qf_ready, m + 1)
            else:
                await_read(eng, ("q", m))

        def place_query(eng, copy, m):
            await_query(eng, m)
            for hh in range(2):
                copy(qz[HD * hh:HD * hh + HD, 2 * m + hh, :], qf[HD * hh:HD * hh + HD, m % 2, 0:NPT]).then_inc(qz_done, 1)

        def place_sample_out(eng, copy, quad, g):
            name = ("so", quad, g)
            ps = await_fill(eng, name)
            last = None
            for hh in range(2):
                rows = slice(HD * hh, HD * hh + HD)
                for r0, r1 in ((0, 4),) if g == 0 else ((0, 2), (2, 4)):
                    b0 = 4 * quad + (r0 - 2 * g) % 4
                    src = ps[rows, :].rearrange("p (j r i x) -> p j r i x", j=4, r=4, i=4)
                    for j in range(4):
                        last = copy(aT[rows, 4 * g + j, NPT + 4 * b0:NPT + 4 * (b0 + r1 - r0)].rearrange("p (r q) -> p r q", q=4),
                                    src[:, j, r0:r1, j, 4 * hh:4 * hh + 4])
            last.then_inc(read_sem(name), 1)

        def place_mem_out(eng, copy, quad, f):
            name = ("mso", quad, f)
            ps = await_fill(eng, name)
            src = ps[:, :].rearrange("p (k r x) -> p k r x", k=4, r=4)
            last = None
            for hl in range(2):
                h = 2 * f + hl
                for r0, r1 in ((0, 4),) if f == 0 else ((0, 2), (2, 4)):
                    b0 = 4 * quad + (r0 - 2 * f) % 4
                    for k in range(2):
                        last = copy(oT[:, 4 * f + 2 * hl + k, NPT + 4 * b0:NPT + 4 * (b0 + r1 - r0)].rearrange("p (r q) -> p r q", q=4),
                                    src[:, 2 * hl + k, r0:r1, 4 * h:4 * h + 4])
            last.then_inc(read_sem(name), 1)

        def eps_col(eps, rows=P):
            i = 0 if eps == LN_EPS else 1
            return eps_small[0:rows, i:i + 1]

        slot_of, loads_of = {}, {}
        count = [0] * EARLY
        for i, item in enumerate(ITEMS):
            slot_of[item] = i % EARLY
            count[i % EARLY] += 32 if item[0] in ("ck", "cv") else 16
            loads_of[item] = count[i % EARLY]

        def item_ap(item):
            s = slot(slot_of[item])
            if item[0] == "w":
                return s.rearrange("p (k n) -> p k n", k=KB)
            if item[0] == "xs":
                return s[0:NS, 0:D]
            return s.rearrange("p (c n) -> p c n", c=2)

        def w_view(ap, col):
            return ap[:, col:col + 256].rearrange("(k p) n -> p k n", p=P)

        win, wmkv = A["w_in"][0], A["w_mkv"][0]
        W_SRC = {
            "k": lambda i: w_view(win, 512 + 256 * i if i < 2 else 2048 + 256 * (i - 2)),
            "q": lambda i: w_view(win, 256 * i if i < 2 else 1536 + 256 * (i - 2)),
            "v": lambda i: w_view(win, 1024 + 256 * i if i < 2 else 2560 + 256 * (i - 2)),
            "mk": lambda i: w_view(wmkv, 256 * i),
            "mv": lambda i: w_view(wmkv, D + 256 * i),
            "o": lambda i: w_view(A["w_out"][0], 256 * i),
            "mq": lambda i: w_view(A["w_mq"][0], 256 * i),
            "mo": lambda i: w_view(A["w_mo"][0], 256 * i),
        }
        halves = lambda ap: ap.rearrange("(c p) n -> p c n", p=P)

        def gu_src(e, k):
            return A["w_gu"][0, bass.ds(e, 1), P * k:P * k + P, :].rearrange("a p n -> p (a n)")

        def dn_src(e, j):
            return A["w_down"][0, bass.ds(e, 1), 256 * j:256 * j + 256, :].rearrange("a (r p) n -> p (a r) n", p=P)

        block = ctx.enter_context(nc.Block())

        @block.tensor
        def _(pe):
            def open_fill(name):
                n = len(fills)
                fills[name] = n
                if n >= ROT:
                    pe.wait_ge(bank_read[n % ROT], n // ROT)
                return bank[n % ROT], bank_full[n % ROT]

            def arrived(item):
                pe.wait_ge(early_in[slot_of[item]], loads_of[item])
                return item_ap(item)

            def turn_blocks(name, pieces):
                ps, full = open_fill(name)
                at = 0
                for src in pieces:
                    rows, cols = src.shape[0], src.shape[1]
                    last = pe.transpose(ps[0:cols, at:at + rows], src, C("ident", 0, rows, rows))
                    at += rows
                return last, full

            def project_T(name, w, col, src, n):
                ps, full = open_fill(name)
                for k in range(KB):
                    last = pe.matmul(ps[:, 0:n], w[:, k, col:col + P], src[:, k, 0:n], start=(k == 0), stop=(k == KB - 1))
                last.then_inc(full, 1)
                return last

            def project_N(name, w, src, c):
                a, r = CHUNKS[c]
                ps, full = open_fill(name)
                for k in range(KB):
                    last = pe.matmul(ps[0:r, 0:256], src[:, k, a:a + r], w[:, k, :], start=(k == 0), stop=(k == KB - 1))
                last.then_inc(full, 1)
                return last

            def used():
                pe.wait_ge(*last_fill())
                pe.sem_inc(item_used, 1)

            def last_fill():
                n = len(fills) - 1
                return bank_full[n % ROT], n // ROT + 1

            pe.wait_ge(const_in, 16)
            x = arrived(("xp",))
            for c in range(2):
                for j in range(2):
                    last, full = turn_blocks(("x", c, j), [x[:, c, P * b:P * b + P] for b in range(4 * j, 4 * j + 4)])
                    last.then_inc(full, 1)
            used()
            x = arrived(("xs",))
            last, full = turn_blocks(("x", 2, 0), [x[:, P * b:P * b + P] for b in range(KB)])
            last.then_inc(full, 1)
            used()
            pe.wait_ge(vec_in, 16 * 6)
            last, full = turn_blocks(("vec",), [vec_rows[:, :]])
            last.then_inc(full, 1)
            for name in (("x", 0, 0), ("x", 0, 1), ("x", 1, 0), ("x", 1, 1), ("x", 2, 0)):
                await_read(pe, name)

            def rotate(kind, m):
                await_read(pe, (kind, m))
                ps, full = open_fill((kind + "r", m))
                pe.matmul(ps[:, 0:T], C("rot"), raw[:, m % 2, :], start=True, stop=True).then_inc(full, 1)

            for kind in "kq":
                for i in range(4):
                    w = arrived(("w", kind, i))
                    for h in range(2):
                        m = 2 * i + h
                        project_T((kind, m), w, P * h, xT, T)
                        if h == 1:
                            used()
                        if 1 <= m <= 4:
                            rotate(kind, m - 1)
            for i in range(4):
                w = arrived(("w", "v", i))
                for c in range(3):
                    project_N(("v", i, c), w, xT, c)
                used()
            for m in range(4, 8):
                await_read(pe, ("k", m))
            pe.wait_ge(roped, 4)
            for c, (a, r) in enumerate(CHUNKS):
                for j in range(2):
                    last, full = turn_blocks(("ko", c, j), [kT[:, b, a:a + r] for b in range(4 * j, 4 * j + 4)])
                    last.then_inc(full, 1)

            def score(p):
                ps, full = open_fill(("s0", p))
                for hh in range(2):
                    last = pe.matmul(ps[:, P * hh:P * hh + P], qz[:, 2 * p + hh, 0:P], kT[:, p, 0:P], start=True, stop=True)
                last.then_inc(full, 1)
                ps, full = open_fill(("s1", p))
                for hh in range(2):
                    last = pe.matmul(ps[:, 256 * hh:256 * hh + 256], qz[:, 2 * p + hh, P:256], kT[:, p, 0:256], start=True, stop=True)
                last.then_inc(full, 1)

            def turn_probs(n, p):
                pe.wait_ge(prob_ready if p < 4 else stick_ready, n // 2 + 1)
                src = tmp[1] if p < 4 else tmp[6]
                for hh in range(2):
                    last, full = turn_blocks(("t", p, hh), [src[:, 384 * hh + P * j:384 * hh + P * j + P] for j in range(3)])
                    last.then_inc(full, 1)

            def attend(n, p):
                await_read(pe, ("t", p, 0))
                await_read(pe, ("t", p, 1))
                ps, full = open_fill(("o", p))
                for kc in range(2):
                    for hh in range(2):
                        pt = ptb[n % 2][hh]
                        v = V[:, kc, P * p + HD * hh:P * p + HD * hh + HD]
                        if kc == 0:
                            last = pe.matmul(ps[HD * hh:HD * hh + HD, 0:256], v, pt[:, 0:256], start=True, stop=False)
                        else:
                            last = pe.matmul(ps[HD * hh:HD * hh + HD, P:256], v, pt[:, 256:384], start=False, stop=True)
                last.then_inc(full, 1)

            pe.wait_ge(qz_done, 2 * NPAIR)
            for i in range(4):
                for c in range(3):
                    await_read(pe, ("v", i, c))
            score(PAIR_ORDER[0])
            score(PAIR_ORDER[1])
            x = arrived(("mem",))
            for c in range(2):
                for j in range(2):
                    last, full = turn_blocks(("m", c, j), [x[:, c, P * b:P * b + P] for b in range(4 * j, 4 * j + 4)])
                    last.then_inc(full, 1)
            used()
            for c in range(2):
                for j in range(2):
                    await_read(pe, ("m", c, j))
            for n, p in enumerate(PAIR_ORDER):
                turn_probs(n, p)
                if n + 2 < NPAIR:
                    score(PAIR_ORDER[n + 2])
                if n % 2 == 0:
                    w = arrived(("w", "mv", n // 2))
                    project_N(("mv", n // 2, 0), w, memT, 0)
                else:
                    project_N(("mv", n // 2, 1), w, memT, 1)
                    used()
                attend(n, p)

            S_BANK, O_BANK = (4, 5), (6, 7)

            def turn_keys(b, kind="ck"):
                x = arrived((kind, b))
                for j in range(4):
                    last, full = turn_blocks((kind, b, j), [x[:, c, P * q:P * q + P] for q in (2 * j, 2 * j + 1) for c in range(2)])
                    last.then_inc(full, 1)
                used()

            def score_pair(b0):
                for b in (b0, b0 + 1):
                    for j in range(4):
                        await_read(pe, ("ck", b, j))
                if b0 == 0:
                    pe.wait_ge(new_keys, 2)
                    pe.wait_ge(qx_done, 2 * NPAIR)
                if b0 == 4:
                    for g in range(2):
                        pe.wait_ge(scores_read[g], 1)
                for j in range(4):
                    for g in range(2):
                        for b in (b0, b0 + 1):
                            r = (b + 2 * g) % 4
                            last = pe.matmul(bank[S_BANK[g]][32 * r:32 * r + 32, 0:T], qx[:, b * NPAIR + 4 * g + j, :],
                                             ktb[b % 2][:, 4 * g + j, :], start=(j == 0), stop=(j == 3))
                last.then_inc(s_scored, 1)

            def turn_sample_probs(quad):
                for g in range(2):
                    pe.wait_ge(s_stick if g else s_prob, quad + 1)
                    src = tmp[1] if g == 0 else tmp[6]
                    last, full = turn_blocks(("st", quad, g), [src[:, 0:P], src[:, P:256], src[:, 256:288]])
                    last.then_inc(full, 1)

            def attend_pair(b0):
                quad = b0 // 4
                if b0 % 4 == 0:
                    for g in range(2):
                        await_read(pe, ("st", quad, g))
                    if quad:
                        for g in range(2):
                            pe.wait_ge(out_read[g], 1)
                vs = [arrived(("cv", b)) for b in (b0, b0 + 1)]
                for kk in range(3):
                    for g in range(2):
                        for b in (b0, b0 + 1):
                            r = (b + 2 * g) % 4
                            v = vs[b - b0][:, kk, 512 * g:512 * g + 512] if kk < 2 else V[:, 2, 512 * g:512 * g + 512]
                            last = pe.matmul(bank[O_BANK[g]][32 * r:32 * r + 32, :], ptq[g][:, kk, 32 * r:32 * r + 32], v,
                                             start=(kk == 0), stop=(kk == 2))
                last.then_inc(s_pv, 1)
                pe.wait_ge(s_pv, b0 // 2 + 1)
                pe.sem_inc(item_used, 2)

            def turn_sample_out(quad):
                for g in range(2):
                    pe.wait_ge(out_read[g], quad + 1)
                    src = so[g]
                    last, full = turn_blocks(("so", quad, g), [src[:, P * j:P * j + P] for j in range(4)])
                    last.then_inc(full, 1)

            turn_keys(0)
            turn_keys(1)
            score_pair(0)
            turn_keys(2)
            turn_keys(3)
            score_pair(2)
            turn_keys(4)
            turn_keys(5)
            turn_sample_probs(0)
            score_pair(4)
            attend_pair(0)
            attend_pair(2)
            turn_keys(6)
            turn_keys(7)
            score_pair(6)
            turn_sample_out(0)
            turn_sample_probs(1)
            attend_pair(4)
            attend_pair(6)
            turn_sample_out(1)

            for g in range(2):
                pe.wait_ge(sq_ready, g + 1)
                ps, full = open_fill(("rms", g))
                for j in range(4):
                    last = pe.matmul(ps[:, 0:T], C("one512"), sqT[:, 4 * g + j, :], start=(j == 0), stop=(j == 3))
                last.then_inc(full, 1)

            def mean_fill(n, kind):
                ps, full = open_fill(("mean", n))
                for m in range(KB):
                    await_read(pe, (kind, m))
                    last = pe.matmul(ps[:, 0:T], C("one1024"), yT[:, m, :], start=(m == 0), stop=(m == KB - 1))
                last.then_inc(full, 1)

            def var_fill(n):
                pe.wait_ge(sq_ready, 2 + n + 1)
                ps, full = open_fill(("var", n))
                for m in range(KB):
                    last = pe.matmul(ps[:, 0:T], C("one1024"), sqT[:, m, :], start=(m == 0), stop=(m == KB - 1))
                last.then_inc(full, 1)

            pe.wait_ge(rms_done, KB)
            for i in range(4):
                w = arrived(("w", "o", i))
                for h in range(2):
                    project_T(("y1", 2 * i + h), w, P * h, aT, T)
                used()
            mean_fill(0, "y1")
            for i in range(4):
                w = arrived(("w", "mk", i))
                for h in range(2):
                    project_T(("mk", 2 * i + h), w, P * h, memT, N_MEM)
                used()
                if i == 1:
                    var_fill(0)
            for m in range(KB):
                await_read(pe, ("mk", m))
            for c in range(2):
                for j in range(2):
                    last, full = turn_blocks(("mko", c, j), [mkT[:, b, P * c:P * c + P] for b in range(4 * j, 4 * j + 4)])
                    last.then_inc(full, 1)
            pe.wait_ge(norm_done, KB)
            for i in range(4):
                w = arrived(("w", "mq", i))
                for h in range(2):
                    project_T(("mq", 2 * i + h), w, P * h, x1T, T)
                used()
            for m in range(KB):
                await_read(pe, ("mq", m))

            def mem_score(h):
                ps, full = open_fill(("ms", h))
                for c in range(2):
                    for f in range(2):
                        last = pe.matmul(ps[:, 256 * c:256 * c + 256], mqT[:, 2 * h + f, P * c:P * c + P],
                                         mkT[:, 2 * h + f, :], start=(f == 0), stop=(f == 1))
                last.then_inc(full, 1)

            def mem_turn(h):
                pe.wait_ge(prob_ready, 4 + h + 1)
                src = tmp[2 * (h % 2) + 1]
                last, full = turn_blocks(("mp", h), [src[:, 256 * c + P * kc:256 * c + P * kc + P] for kc in range(2) for c in range(2)])
                last.then_inc(full, 1)

            def mem_attend(h):
                await_read(pe, ("mp", h))
                ps, full = open_fill(("mo", h))
                for f in range(2):
                    for kc in range(2):
                        last = pe.matmul(ps[:, 256 * f:256 * f + 256], mvN[:, kc, 256 * h + P * f:256 * h + P * f + P],
                                         tmp[4 + h % 2][:, 256 * kc:256 * kc + 256], start=(kc == 0), stop=(kc == 1))
                last.then_inc(full, 1)

            def mem_score_pair(b0):
                for b in (b0, b0 + 1):
                    for j in range(4):
                        await_read(pe, ("mk", b, j))
                if b0 == 0:
                    pe.wait_ge(mqx_done, 1)
                for m in range(KB):
                    for b in (b0, b0 + 1):
                        r = b % 4
                        last = pe.matmul(bank[S_BANK[b // 4]][32 * r:32 * r + 32, 0:N_MEM], qx[:, b * KB + m, :],
                                         ktb[b % 2][:, m, 0:N_MEM], start=(m == 0), stop=(m == KB - 1))
                last.then_inc(s_scored, 1)

            def mem_turn_sample(quad):
                pe.wait_ge(s_prob, 2 + quad + 1)
                src = tmp[6 + quad]
                last, full = turn_blocks(("mst", quad), [src[:, 0:P], src[:, P:256]])
                last.then_inc(full, 1)

            def mem_attend_pair(b0):
                quad = b0 // 4
                if b0 % 4 == 0:
                    await_read(pe, ("mst", quad))
                    for f in range(2):
                        pe.wait_ge(out_read[f], 2 + quad)
                vs = [arrived(("mv", b)) for b in (b0, b0 + 1)]
                for kk in range(2):
                    for f in range(2):
                        for b in (b0, b0 + 1):
                            r, rp = (b + 2 * f) % 4, b % 4
                            last = pe.matmul(bank[O_BANK[f]][32 * r:32 * r + 32, :], ptq[quad][:, kk, 32 * rp:32 * rp + 32],
                                             vs[b - b0][:, kk, 512 * f:512 * f + 512], start=(kk == 0), stop=(kk == 1))
                last.then_inc(s_pv, 1)
                pe.wait_ge(s_pv, 4 + b0 // 2 + 1)
                pe.sem_inc(item_used, 2)

            def mem_turn_out(quad):
                for f in range(2):
                    pe.wait_ge(out_read[f], 2 + quad + 1)
                    last, full = turn_blocks(("mso", quad, f), [so[f][:, P * j:P * j + P] for j in range(4)])
                    last.then_inc(full, 1)

            mem_score(0)
            mem_score(1)
            turn_keys(0, "mk")
            for h in range(4):
                mem_turn(h)
                if h + 2 < 4:
                    mem_score(h + 2)
                mem_attend(h)
            turn_keys(1, "mk")
            mem_score_pair(0)
            for b0 in (2, 4, 6):
                turn_keys(b0, "mk")
                turn_keys(b0 + 1, "mk")
                mem_score_pair(b0)
            mem_turn_sample(0)
            mem_attend_pair(0)
            mem_attend_pair(2)
            mem_turn_sample(1)
            mem_turn_out(0)
            mem_attend_pair(4)
            mem_attend_pair(6)
            mem_turn_out(1)

            for h in range(4):
                await_read(pe, ("mo", h))
            for quad in range(2):
                for f in range(2):
                    await_read(pe, ("mso", quad, f))
            for i in range(4):
                w = arrived(("w", "mo", i))
                for h in range(2):
                    project_T(("y2", 2 * i + h), w, P * h, oT, T)
                used()
            mean_fill(1, "y2")
            var_fill(1)
            pe.wait_ge(norm_done, 2 * KB)

            pe.wait_ge(late_in, 16 * 8)
            ps, full = open_fill(("lgT",))
            for k in range(KB):
                last = pe.matmul(ps[0:NE, 0:T], w_router[:, k, :], x2T[:, k, :], start=(k == 0), stop=(k == KB - 1))
            last.then_inc(full, 1)
            for c, (a, r) in enumerate(CHUNKS):
                for j in range(2):
                    last, full = turn_blocks(("tok", c, j), [x2T[:, b, a:a + r] for b in range(4 * j, 4 * j + 4)])
                    last.then_inc(full, 1)
            pe.wait_ge(*last_fill())
            pe.sem_inc(x2_used, 1)
            await_read(pe, ("lgT",))
            ps, full = open_fill(("lg",))
            for c, (a, r) in enumerate(CHUNKS):
                last = pe.transpose(ps[0:r, NE * c:NE * c + NE], logT[0:NE, a:a + r], C("ident", 0, NE, NE))
            last.then_inc(full, 1)
            pe.wait_ge(route_ready, 1)
            ps, full = open_fill(("rank",))
            for c in range(3):
                for d in range(c + 1):
                    pe.matmul(ps[:, NE * c:NE * c + NE], C("tri") if d == c else C("one"), mask[:, d, :], start=(d == 0), stop=(d == c))
            for d in range(3):
                last = pe.matmul(ps[:, 96:128], C("one"), mask[:, d, :], start=(d == 0), stop=(d == 2))
            last.then_inc(full, 1)
            ps, full = open_fill(("gT",))
            for c, (a, r) in enumerate(CHUNKS):
                last = pe.transpose(ps[0:NE, a:a + r], gates[0:r, c, :], C("ident", 0, r, r))
            last.then_inc(full, 1)
            await_read(pe, ("gT",))
            pe.wait_ge(zeroed, 17)
            for c, (a, r) in enumerate(CHUNKS):
                for h in range(2):
                    ps, full = open_fill(("bd", c, h))
                    pe.matmul(ps[0:r, :], gT[:, a:a + r], bdown[:, 512 * h:512 * h + 512], start=True, stop=True).then_inc(full, 1)
            pe.wait_ge(moe_ready, 3)
            for c in range(3):
                for h in range(2):
                    await_read(pe, ("bd", c, h))

            blocks_done = pe.alloc_register("pe_blocks")
            pe.reg_mov(blocks_done, 0)
            pe.sem_inc(sel_turned, 1)
            COMB_BANK = (6, 7, 5, 4, 0)

            def combine():
                for c in range(2):
                    for h in range(2):
                        pe.matmul(bank[COMB_BANK[2 * c + h]][:, :], selT[h][:, P * c:P * c + P], y_s[:, :],
                                  start=True, stop=True).then_inc(comb, 1)
                for h in range(2):
                    last = pe.matmul(bank[COMB_BANK[4]][32 * h:32 * h + 32, :], selT[h][:, 256:T], y_s[:, :], start=True, stop=True)
                last.then_inc(comb, 1)

            def expert_block(e, release):
                n = pe.snap(blocks_done)
                pe.wait_ge(sel_ready, n + 1)
                pe.wait_ge(added, n * 5 + 1)
                for m in range(KB):
                    for c in range(3):
                        for part in range(3):
                            last = pe.matmul(bank[0][:, CAP * m:CAP * m + CAP], tokn[:, part, c, P * m:P * m + P], pick[:, c, :],
                                             start=(c == 0 and part == 0), stop=(c == 2 and part == 2))
                last.then_inc(picked, 1)
                for j in range(2):
                    for h in range(2):
                        pe.matmul(bank[1 + j][64 * h:64 * h + 64, :], ebias[0:96, :], bgu[:, D * j + 512 * h:D * j + 512 * h + 512],
                                  start=True, stop=False)
                pe.wait_ge(xg_ready, n + 1)
                for k in range(KB):
                    pe.wait_ge(expert_in[k], 16 * e + 16)
                    w = slot(k)
                    for j in range(2):
                        for h in range(2):
                            last = pe.matmul(bank[1 + j][64 * h:64 * h + 64, :], xgT[:, k, :], w[:, D * j + 512 * h:D * j + 512 * h + 512],
                                             start=False, stop=(k == KB - 1))
                    if release and k < KB - 1:
                        last.then_inc(chunk_used, 1)
                last.then_inc(gu_done, 1)
                pe.wait_ge(y_ready, n + 1)
                pe.wait_ge(selT_ready, n + 1)
                combine()
                if release:
                    pe.wait_ge(gu_done, n + 1)
                    pe.sem_inc(chunk_used, 1)
                pe.wait_ge(act_ready, n + 1)
                for j in range(4):
                    last = pe.transpose(bank[3][:, P * j:P * j + P], act_s[:, P * j:P * j + P], C("ident"))
                last.then_inc(act_turned, 1)
                pe.wait_ge(added, n * 5 + 5)
                for c, (a, r) in enumerate(CHUNKS):
                    last = pe.transpose(bank[5][:, a:a + r], gpick[0:r, c, :], C("ident", 0, r, r))
                last.then_inc(sel_turned, 1)
                pe.wait_ge(actT_ready, n + 1)
                for i in range(4):
                    pe.wait_ge(expert_in[KB + i], 16 * e + 16)
                    w = slot(KB + i).rearrange("p (r n) -> p r n", r=2)
                    for r in range(2):
                        f = 2 * i + r
                        for h in range(2):
                            last = pe.matmul(bank[4][64 * h:64 * h + 64, :], actT[:, f % 4, 64 * (f // 4):64 * (f // 4) + 64],
                                             w[:, r, 512 * h:512 * h + 512], start=(f == 0), stop=(f == KB - 1))
                    if release and i < 3:
                        last.then_inc(chunk_used, 1)
                last.then_inc(down_done, 1)
                if release:
                    pe.wait_ge(down_done, n + 1)
                    pe.sem_inc(chunk_used, 1)
                pe.reg_add(blocks_done, blocks_done, 1)

            with pe.Fori(0, NE) as e:
                more = pe.value_load(nextra[0:1, bass.ds(e, 1)], min_val=0, max_val=4)
                with pe.If(more > 0):
                    with pe.Fori(0, more):
                        expert_block(e, False)
                expert_block(e, True)
            n = pe.snap(blocks_done)
            pe.wait_ge(y_ready, n + 1)
            pe.wait_ge(selT_ready, n + 1)
            pe.wait_ge(added, n * 5 + 1)
            combine()

        @block.sync
        def _(sp):
            sp.dma_start(consts[:, :], A["consts"]).then_inc(const_in, 16)
            sp.dma_start(pages[0:1, :], A["page_table"].rearrange("(a b) g -> a (b g)", a=1)).then_inc(pages_in, 16)

            def early(i):
                item = ITEMS[i]
                if i >= EARLY:
                    sp.wait_ge(item_used, i - EARLY + 1)
                dst, s = item_ap(item), early_in[slot_of[item]]
                if item[0] == "xp":
                    sp.dma_start(dst, halves(A["x_prompt"][0])).then_inc(s, 16)
                elif item[0] == "xs":
                    sp.dma_start(dst, A["x_sample"].rearrange("b q n -> (b q) n")).then_inc(s, 16)
                elif item[0] == "mem":
                    sp.dma_start(dst, halves(A["mem_prompt"][0])).then_inc(s, 16)
                elif item[0] == "w":
                    sp.dma_start(dst, W_SRC[item[1]](item[2])).then_inc(s, 16)
                elif item[0] in ("ck", "cv"):
                    src = A["cache_k" if item[0] == "ck" else "cache_v"]
                    if item == ("ck", 0):
                        sp.wait_ge(pages_in, 16)
                    for g in range(PAGES):
                        at = item[1] * PAGES + g
                        page = sp.value_load(pages[0:1, at:at + 1], min_val=0, max_val=N_PHYS - 1)
                        sp.dma_start(dst[:, g, :], src[0, bass.ds(page, 1)].rearrange("a t h d -> t (a h d)")).then_inc(s, 16)
                else:
                    src = A["cache_mem_k" if item[0] == "mk" else "cache_mem_v"]
                    sp.dma_start(dst, src[0, item[1]].rearrange("(c p) h d -> p c (h d)", p=P)).then_inc(s, 16)

            for i in range(len(ITEMS)):
                early(i)

            def chunk(e, j):
                if j < KB:
                    sp.dma_start(slot(j), gu_src(e, j)).then_inc(expert_in[j], 16)
                else:
                    sp.dma_start(slot(j).rearrange("p (r n) -> p r n", r=2), dn_src(e, j - KB)).then_inc(expert_in[j], 16)

            for j in range(RING):
                if j < EARLY:
                    last = max(i for i in range(len(ITEMS)) if i % EARLY == j)
                    sp.wait_ge(item_used, last + 1)
                elif j == EARLY:
                    sp.wait_ge(x2_used, 1)
                chunk(0, j)
            with sp.Fori(1, NE) as e:
                for j in range(RING):
                    sp.wait_ge(chunk_used, RING * e - RING + j + 1)
                    chunk(e, j)

        @block.gpsimd
        def _(pool):
            done = [0]

            def step(ins):
                done[0] += 1
                ins.then_inc(pool_step, 1)

            def settle():
                pool.wait_ge(pool_step, done[0])

            rows = [("g_moba", 0, 4), ("g_sb", 4, 4), ("ln1_g", 8, 8), ("ln1_b", 16, 8), ("ln2_g", 24, 8), ("ln2_b", 32, 8)]
            for name, at, n in rows:
                pool.dma_start(vec_rows[at:at + n, :], A[name][0].rearrange("(a p) -> a p", p=P)).then_inc(vec_in, 16)
            cleared = [0]

            def clear(view, value=0.0):
                pool.memset(view, value).then_inc(zeroed, 1)
                cleared[0] += 1
                pool.wait_ge(zeroed, cleared[0])

            clear(qz)
            clear(qx)
            clear(V[32:64, 2, :])
            clear(V[64:128, 2, :])

            def spread(src, m, sem_out):
                for hh in range(2):
                    at = (m % 4) * 8 + hh * 4
                    if m or hh:
                        pool.wait_ge(sem_out, 2 * m + hh)
                    out = qx[HD * hh:HD * hh + HD, :, at:at + 4].rearrange("p (b g) q -> p b g q", b=NB_DEC)[:, :, m, :]
                    pool.tensor_copy(out, src[HD * hh:HD * hh + HD, NPT:T].rearrange("p (b q) -> p b q", q=Q_DEC)).then_inc(sem_out, 1)

            pool.wait_ge(zeroed, 4)
            for m in range(NPAIR):
                await_query(pool, m)
                spread(qf[:, m % 2, :], m, qx_done)

            for i in range(4):
                for c in range(3):
                    await_read(pool, ("v", i, c))
            pool.dma_start(halves(O["new_v_prompt"]), V[:, 0:2, :]).then_inc(kv_stored, 16)
            pool.dma_start(O["new_v_sample"], V[0:NS, 2, :]).then_inc(kv_stored, 16)
            for c in range(3):
                for j in range(2):
                    await_read(pool, ("ko", c, j))
            pool.dma_start(halves(O["new_k_prompt"]), knat[:, 0:2, :]).then_inc(kv_stored, 16)
            pool.dma_start(O["new_k_sample"], knat[0:NS, 2, :]).then_inc(kv_stored, 16)
            for i in range(4):
                for c in range(2):
                    await_read(pool, ("mv", i, c))
            pool.dma_start(halves(O["mem_v_prompt"]), mvN).then_inc(stored, 16)

            await_fill(pool, ("o", PAIR_ORDER[-1]))
            await_fill(pool, ("o", PAIR_ORDER[-2]))
            for g in range(2):
                for a, b in ((32, 64), (64, 128)):
                    clear(ptq[g][a:b, 2, :])

            pool.wait_ge(s_scored, 4)
            clear(qx)
            pool.dma_start(w_router, A["w_router"][0].rearrange("(k p) n -> p k n", p=P)).then_inc(late_in, 16)
            pool.dma_start(b_router, A["b_router"].rearrange("a e -> e a")).then_inc(late_in, 16)
            for c in range(2):
                for j in range(2):
                    await_read(pool, ("mko", c, j))
            pool.dma_start(halves(O["mem_k_prompt"]), mknat).then_inc(stored, 16)
            pool.wait_ge(zeroed, 9)
            for m in range(KB):
                await_read(pool, ("mq", m))
            for m in range(KB):
                h = m // 2
                out = qx[:, :, 4 * h:4 * h + 4].rearrange("p (b g) q -> p b g q", b=NB_DEC)[:, :, m, :]
                last = pool.tensor_copy(out, mqT[:, m, NPT:T].rearrange("p (b q) -> p b q", q=Q_DEC))
            last.then_inc(mqx_done, 1)
            for quad in range(2):
                for f in range(2):
                    await_read(pool, ("mso", quad, f))
            for h in range(4):
                await_read(pool, ("mo", h))
            clear(bdown[32:64, :])
            clear(bdown[64:128, :])
            pool.dma_start(bdown[0:NE, :], A["b_down"][0]).then_inc(late_in, 16)
            pool.wait_ge(stored, 16 * 2)
            clear(topf, -1.0)
            clear(gk)
            for part in range(3):
                pool.dma_start(bgu_f[32 * part:32 * part + 32, :], A["b_gu"][0]).then_inc(late_in, 16)
            pool.dma_start(ln3[:, 0, :], A["ln3_g"].broadcast_to([P, D])).then_inc(late_in, 16)
            pool.dma_start(ln3[:, 1, :], A["ln3_b"].broadcast_to([P, D])).then_inc(late_in, 16)

            await_fill(pool, ("var", 1))
            for a, b in ((32, 64), (64, 128)):
                clear(tokn[a:b, :, 2, :])
                clear(gT[a:b, :])
            for i in range(2):
                clear(selT[i])
            clear(y_s)
            for i in range(3):
                step(pool.tensor_copy(ebias_src[32 * i:32 * i + 32, :], C("eye3", 0, 32)[32 * i:32 * i + 32, :]))
                settle()
            pool.sem_inc(moe_ready, 1)
            pool.wait_ge(moe_ready, 3)
            blocks_done = pool.alloc_register("pool_blocks")
            pool.reg_mov(blocks_done, 0)
            base = done[0]

            def expert_block(e, first_slot):
                n = pool.snap(blocks_done)
                pool.wait_ge(sel_turned, n + 1)
                pool.wait_ge(pool_step, n * 10 + base)
                pool.wait_ge(moe_ready, 3)
                pool.tensor_copy(rcol, rankm[:, :, bass.ds(e, 1)].rearrange("p c a -> p (c a)")).then_inc(pool_step, 1)
                pool.tensor_copy(gcol, gates[:, :, bass.ds(e, 1)].rearrange("p c a -> p (c a)")).then_inc(pool_step, 1)
                if first_slot is None:
                    pool.tensor_copy(slots_now, C("slot2")).then_inc(pool_step, 1)
                else:
                    pool.tensor_copy(slots_now.rearrange("p (a b) -> p a b", a=2),
                                     C("iota")[:, bass.ds(first_slot, CAP)].rearrange("p (a b) -> p a b", a=1).broadcast_to([P, 2, CAP])).then_inc(pool_step, 1)
                pool.tensor_copy(ebias[0:96, :], ebias_src[0:96, bass.ds(e, 1)].broadcast_to([96, CAP])).then_inc(pool_step, 1)
                pool.wait_ge(pool_step, n * 10 + base + 4)
                pool.sem_inc(tables_in, 1)
                for c in range(3):
                    pool.tensor_scalar(pick[:, c, :], slots_now[:, 0:CAP], rcol[:, c:c + 1], None, ALU.is_equal).then_inc(pool_step, 1)
                    pool.tensor_scalar(gpick[:, c, :], slots_now, rcol[:, c:c + 1], gcol[:, c:c + 1], ALU.is_equal, ALU.mult).then_inc(pool_step, 1)
                pool.wait_ge(pool_step, n * 10 + base + 10)
                pool.sem_inc(sel_ready, 1)
                pool.reg_add(blocks_done, blocks_done, 1)

            with pool.Fori(0, NE) as e:
                more = pool.value_load(nextra[0:1, bass.ds(e, 1)], min_val=0, max_val=4)
                with pool.If(more > 0):
                    with pool.Fori(0, more) as i:
                        expert_block(e, i * CAP + CAP)
                expert_block(e, None)

            pool.wait_ge(fin_ready, 3)
            pool.dma_start(halves(O["y_prompt"]), acc[:, 0:2, :]).then_inc(stored, 16)
            pool.dma_start(O["y_sample"], acc[0:NS, 2, :]).then_inc(stored, 16)
            pool.wait_ge(kv_stored, 16 * 4)
            pool.wait_ge(stored, 16 * 4)

        @block.scalar
        def _(act):
            done, exps, sticks = [0], [0], [0]

            def step(ins):
                done[0] += 1
                ins.then_inc(act_step, 1)

            def settle():
                act.wait_ge(act_step, done[0])

            def copy(out, in_, scale=1.0):
                return act.activation(out, in_, ACT.Copy, scale=scale)

            def carry(name, out, view):
                copy(out, view(await_fill(act, name))).then_inc(read_sem(name), 1)

            def wide(n):
                return lambda ps: ps[:, 0:n]

            def by(count, n, rows=P):
                return lambda ps: ps[0:rows, 0:count * n].rearrange("p (a b) -> p a b", b=n)

            carry(("x", 0, 1), xT[:, 4:8, 0:128], by(4, P))
            carry(("x", 1, 1), xT[:, 4:8, 128:256], by(4, P))
            carry(("vec",), vec[:, :], wide(40))

            act.wait_ge(zeroed, 4)
            for kind in "kq":
                for m in range(NPAIR):
                    if m < 4:
                        if m >= 2:
                            await_read(act, (kind + "r", m - 2))
                        elif kind == "q":
                            await_read(act, ("kr", m + 2))
                        carry((kind, m), raw[:, m % 2, :], wide(T))
                    elif kind == "k":
                        carry((kind, m), kT[:, m, :], wide(T))
                    if kind == "q" and m >= 1:
                        place_query(act, copy, m - 1)
            place_query(act, copy, NPAIR - 1)
            act.wait_ge(roped, 4)
            for m in range(4, NPAIR):
                await_read(act, ("k", m))
            for i in range(2):
                copy(ktb[i][:, :, PAST:T], kT[:, :, NPT:T]).then_inc(new_keys, 1)
            for i in range(4):
                for c in (0, 2):
                    r = CHUNKS[c][1]
                    carry(("v", i, c), V[0:r, c, 256 * i:256 * i + 256], lambda ps: ps[0:r, 0:256])
            for c, (a, r) in enumerate(CHUNKS):
                carry(("ko", c, 1), knat[0:r, c, 512:D], lambda ps: ps[0:r, :])

            def softmax_exp(s, p, parts, at):
                exps[0] += 1
                act.wait_ge(max_ready, exps[0])
                for i, (a, b, rows) in enumerate(parts):
                    last = act.activation(p[:, a:b], s[:, a:b], ACT.Exp, bias=small[:, at + 4 + i:at + 5 + i],
                                          accum_out=small[:, at + 8 + i:at + 9 + i])
                last.then_inc(exp_ready, 1)

            PARTS = [(0, 128, P), (384, 512, P), (128, 384, P), (512, 768, P)]

            def stick_logs(z, t, n):
                settle()
                step(act.activation(t[:, 0:n], z[:, 0:n], ACT.Abs))
                settle()
                step(act.activation(t[:, 0:n], t[:, 0:n], ACT.Exp, scale=-1.0))
                settle()
                act.activation(t[:, 0:n], t[:, 0:n], ACT.Ln, bias=1.0).then_inc(log_ready, 1)

            def prompt_stick(n):
                p = PAIR_ORDER[n]
                z = tmp[2].rearrange("p (h n) -> p h n", h=2)
                if n >= 2:
                    act.wait_ge(arg_ready, sticks[0])
                ps = await_fill(act, ("s0", p))
                copy(z[:, :, 0:P], ps[:, 0:256].rearrange("p (h n) -> p h n", h=2), ATT_SCALE).then_inc(read_sem(("s0", p)), 1)
                ps = await_fill(act, ("s1", p))
                copy(z[:, :, P:384], ps[:, :].rearrange("p (h n) -> p h n", h=2), ATT_SCALE).then_inc(read_sem(("s1", p)), 1)
                await_read(act, ("s0", p))
                await_read(act, ("s1", p))
                stick_logs(tmp[2], tmp[3], 768)

            def prompt_stick_exp(n):
                sticks[0] += 1
                act.wait_ge(arg_ready, sticks[0])
                if n >= 2:
                    await_fill(act, ("t", PAIR_ORDER[n - 2], 1))
                act.activation(tmp[6], tmp[4], ACT.Exp).then_inc(stick_ready, 1)

            def prompt_exp(n):
                if n >= 2:
                    await_fill(act, ("t", PAIR_ORDER[n - 2], 1))
                softmax_exp(tmp[0], tmp[1], PARTS, 0)

            prompt_exp(0)
            prompt_stick(1)
            act.wait_ge(kv_stored, 16 * 4)
            for c in range(2):
                carry(("m", c, 1), memT[:, 4:8, P * c:P * c + P], by(4, P))
            for n, p in enumerate(PAIR_ORDER):
                if n % 2 == 0:
                    prompt_stick_exp(n + 1)
                if n >= 2:
                    await_fill(act, ("o", PAIR_ORDER[n - 2]))
                carry(("t", p, 0), ptb[n % 2][0], wide(384))
                if n + 2 < NPAIR:
                    if n % 2 == 0:
                        prompt_exp(n + 2)
                    else:
                        prompt_stick(n + 2)
                if n % 2 == 0:
                    carry(("mv", n // 2, 0), mvN[:, 0, 128 * n:128 * n + 256], wide(256))

            def keys_in(kind, b):
                if kind == "ck" and b >= 2:
                    act.wait_ge(s_scored, b // 2)
                if kind == "mk":
                    act.wait_ge(s_scored, 4 + b // 2)
                for j in (1, 3):
                    carry((kind, b, j), ktb[b % 2][:, 2 * j:2 * j + 2, 0:PAST], by(2, 256))

            def sample_stick(quad):
                act.wait_ge(s_scored, 2 * quad + 2)
                if quad == 0:
                    act.wait_ge(arg_ready, sticks[0])
                copy(tmp[2][:, 0:T], bank[5][:, 0:T], ATT_SCALE).then_inc(scores_read[1], 1)
                act.wait_ge(scores_read[1], quad + 1)
                stick_logs(tmp[2], tmp[3], T)

            def sample_stick_exp(quad):
                sticks[0] += 1
                act.wait_ge(arg_ready, sticks[0])
                if quad:
                    await_fill(act, ("st", quad - 1, 1))
                else:
                    await_fill(act, ("t", PAIR_ORDER[-1], 1))
                act.activation(tmp[6][:, 0:T], tmp[4][:, 0:T], ACT.Exp).then_inc(s_stick, 1)

            def sample_exp(quad):
                if quad:
                    await_fill(act, ("st", quad - 1, 0))
                else:
                    await_fill(act, ("t", PAIR_ORDER[-2], 1))
                softmax_exp(tmp[0], tmp[1], [(0, T, P)], 0)

            def sample_probs_in(quad):
                if quad == 0:
                    act.wait_ge(zeroed, 8)
                    await_fill(act, ("o", PAIR_ORDER[-1]))
                else:
                    act.wait_ge(s_pv, 2)
                ps = await_fill(act, ("st", quad, 0))
                copy(ptq[0][:, 0:2, :], ps[:, 0:256].rearrange("p (a b) -> p a b", b=P))
                copy(ptq[0][0:NS, 2, :], ps[0:NS, 256:384]).then_inc(read_sem(("st", quad, 0)), 1)

            def out_in(quad, f, n_pv, before):
                act.wait_ge(s_pv, n_pv)
                if before is not None:
                    await_fill(act, before)
                copy(so[0], bank[6][:, :]).then_inc(out_read[0], 1)

            keys_in("ck", 0)
            keys_in("ck", 1)
            keys_in("ck", 2)
            keys_in("ck", 3)
            sample_stick(0)
            keys_in("ck", 4)
            sample_exp(0)
            keys_in("ck", 5)
            sample_stick_exp(0)
            sample_probs_in(0)
            out_in(0, 0, 2, None)
            keys_in("ck", 6)
            keys_in("ck", 7)
            sample_stick(1)
            place_sample_out(act, copy, 0, 0)
            sample_exp(1)
            sample_stick_exp(1)
            sample_probs_in(1)
            out_in(1, 0, 4, ("so", 0, 0))
            place_sample_out(act, copy, 1, 0)

            for p in range(NPAIR):
                await_read(act, ("o", p))
            act.wait_ge(s_scored, 4)
            for g in range(2):
                for quad in range(2):
                    await_read(act, ("so", quad, g))
                act.activation(sqT[:, 4 * g:4 * g + 4, :], aT[:, 4 * g:4 * g + 4, :], ACT.Square).then_inc(sq_ready, 1)

            def inverse_root(name, eps, out, tmp_, sem_out, ready):
                if ready:
                    act.wait_ge(ready[0], ready[1])
                ps = await_fill(act, name)
                act.activation(tmp_, ps[:, 0:T], ACT.Ln, bias=eps_col(eps)).then_inc(read_sem(name), 1)
                await_read(act, name)
                act.activation(out, tmp_, ACT.Exp, scale=-0.5).then_inc(sem_out, 1)

            act.wait_ge(eps_ready, 2)
            for g in range(2):
                inverse_root(("rms", g), RMS_EPS, rstd, lnv, rstd_ready, (rms_done, 4) if g else None)

            def layer_norm(n, out, beta):
                for h in range(2):
                    act.wait_ge(centered, 2 * n + h + 1)
                    last = act.activation(sqT[:, 4 * h:4 * h + 4, :], yT[:, 4 * h:4 * h + 4, :], ACT.Square)
                last.then_inc(sq_ready, 1)
                if n == 0:
                    mid()
                inverse_root(("var", n), LN_EPS, rstd, lnv, rstd_ready, (rms_done, 8) if n == 0 else (norm_mul, KB))
                for m in range(KB):
                    act.wait_ge(norm_mul, KB * n + m + 1)
                    act.activation(out[:, m, :], yT[:, m, :], ACT.Identity, bias=vec[:, beta + m:beta + m + 1]).then_inc(norm_done, 1)

            def mid():
                for m in range(0, 4):
                    if m % 2 == 0:
                        carry(("mk", m), mkT[:, m, :], wide(N_MEM))

            layer_norm(0, x1T, 16)
            for m in range(4, KB, 2):
                carry(("mk", m), mkT[:, m, :], wide(N_MEM))
            for c in range(2):
                carry(("mko", c, 1), mknat[:, c, 512:D], wide(512))

            for m in range(1, KB, 2):
                carry(("mq", m), mqT[:, m, :], wide(T))

            def mem_exp(h):
                i = 2 * (h % 2)
                if h >= 2:
                    await_fill(act, ("mp", h - 2))
                softmax_exp(tmp[i], tmp[i + 1], [(0, 256, P), (256, 512, P)], 16 * (h % 2))

            def mem_probs_in(h):
                if h >= 2:
                    await_fill(act, ("mo", h - 2))
                carry(("mp", h), tmp[4 + h % 2][:, 0:512], wide(512))

            mem_exp(0)
            mem_exp(1)
            keys_in("mk", 0)
            for h in range(4):
                mem_probs_in(h)
                if h + 2 < 4:
                    mem_exp(h + 2)
            keys_in("mk", 1)

            def mem_sample_exp(quad):
                softmax_exp(tmp[6 + quad], tmp[6 + quad], [(0, 256, P)], 16 * quad)

            def mem_sample_probs_in(quad):
                act.wait_ge(s_pv, 4)
                carry(("mst", quad), ptq[quad][:, 0:2, :], by(2, P))

            keys_in("mk", 2)
            keys_in("mk", 3)
            keys_in("mk", 4)
            keys_in("mk", 5)
            mem_sample_exp(0)
            keys_in("mk", 6)
            keys_in("mk", 7)
            mem_sample_probs_in(0)
            mem_sample_exp(1)
            out_in(0, 0, 6, ("so", 1, 0))
            mem_sample_probs_in(1)
            place_mem_out(act, copy, 0, 0)
            out_in(1, 0, 8, ("mso", 0, 0))
            place_mem_out(act, copy, 1, 0)

            layer_norm(1, x2T, 32)

            act.wait_ge(late_in, 16 * 8)
            ps = await_fill(act, ("lgT",))
            act.activation(logT[0:NE, :], ps[0:NE, 0:T], ACT.Identity, bias=b_router).then_inc(read_sem(("lgT",)), 1)
            for c, (a, r) in enumerate(CHUNKS):
                for j in range(2):
                    carry(("tok", c, j), acc[0:r, c, 512 * j:512 * j + 512], lambda ps: ps[0:r, :])
            act.wait_ge(router_go, 1)
            for c, (a, r) in enumerate(CHUNKS):
                last = act.activation(gk[0:r, c, :], top[0:r, c, 0:TOPK], ACT.Exp, bias=small[0:r, c:c + 1],
                                      accum_out=small[0:r, 4 + c:5 + c])
            last.then_inc(router_exp, 1)
            ps = await_fill(act, ("gT",))
            copy(gT[0:NE, :], ps[0:NE, 0:T]).then_inc(read_sem(("gT",)), 1)
            for h in range(2):
                await_read(act, ("bd", 2, h))
                step(copy(acc2[32 * h:32 * h + 32, :], acc[0:NS, 2, 512 * h:512 * h + 512]))
            settle()
            act.sem_inc(moe_ready, 1)

            act.wait_ge(moe_ready, 3)
            act.sem_inc(y_ready, 1)
            act.sem_inc(selT_ready, 1)
            blocks_done = act.alloc_register("act_blocks")
            act.reg_mov(blocks_done, 0)

            def expert_block():
                n = act.snap(blocks_done)
                act.wait_ge(picked, n + 1)
                copy(xgT, bank[0][:, :].rearrange("p (a b) -> p a b", b=CAP)).then_inc(xg_ready, 1)
                act.wait_ge(sig_in, n + 1)
                act.activation(sig_s, gate_s, ACT.Sigmoid, scale=SW_ALPHA).then_inc(sig_ready, 1)
                act.wait_ge(act_turned, n + 1)
                copy(actT, bank[3][:, :].rearrange("p (a b) -> p a b", b=P)).then_inc(actT_ready, 1)
                act.wait_ge(sel_turned, n + 2)
                copy(selT[0][0:64, :], bank[5][0:64, 0:T])
                copy(selT[1][64:128, :], bank[5][64:128, 0:T]).then_inc(selT_ready, 1)
                act.wait_ge(down_done, n + 1)
                copy(y_s, bank[4][:, :]).then_inc(y_ready, 1)
                act.reg_add(blocks_done, blocks_done, 1)

            with act.Fori(0, NE) as e:
                more = act.value_load(nextra[0:1, bass.ds(e, 1)], min_val=0, max_val=4)
                with act.If(more > 0):
                    with act.Fori(0, more):
                        expert_block()
                expert_block()

            for c, (a, r) in enumerate(CHUNKS):
                act.wait_ge(fin_var, c + 1)
                step(act.activation(small[0:r, 24 + c:25 + c], small[0:r, 17 + 2 * c:18 + 2 * c], ACT.Ln, bias=eps_col(LN_EPS, r)))
                settle()
                act.activation(small[0:r, 24 + c:25 + c], small[0:r, 24 + c:25 + c], ACT.Exp, scale=-0.5).then_inc(fin_rstd, 1)

        @block.vector
        def _(dve):
            done, fronts, exps, logs = [0], [0], [0], [0]

            def step(ins):
                done[0] += 1
                ins.then_inc(dve_step, 1)

            def settle():
                dve.wait_ge(dve_step, done[0])

            copy = dve.tensor_copy

            def carry(name, out, view):
                copy(out, view(await_fill(dve, name))).then_inc(read_sem(name), 1)

            def wide(n):
                return lambda ps: ps[:, 0:n]

            def by(count, n, rows=P):
                return lambda ps: ps[0:rows, 0:count * n].rearrange("p (a b) -> p a b", b=n)

            dve.memset(eps_small[:, 0:1], LN_EPS).then_inc(eps_ready, 1)
            dve.memset(eps_small[:, 1:2], RMS_EPS).then_inc(eps_ready, 1)
            carry(("x", 0, 0), xT[:, 0:4, 0:128], by(4, P))
            carry(("x", 1, 0), xT[:, 0:4, 128:256], by(4, P))
            carry(("x", 2, 0), xT[:, :, NPT:T], by(KB, NS))

            for kind in "kq":
                for m in range(NPAIR):
                    if m < 4:
                        await_read(dve, (kind, m))
                        step(dve.tensor_tensor(rope_t[:, 0, :], raw[:, m % 2, :], C("cos"), ALU.mult))
                        ps = await_fill(dve, (kind + "r", m))
                        dve.tensor_tensor(rope_t[:, 1, :], ps[:, 0:T], C("sin"), ALU.mult).then_inc(read_sem((kind + "r", m)), 1)
                        await_read(dve, (kind + "r", m))
                        settle()
                    if kind == "k":
                        if m < 4:
                            dve.tensor_tensor(kT[:, m, :], rope_t[:, 0, :], rope_t[:, 1, :], ALU.add).then_inc(roped, 1)
                            dve.wait_ge(roped, m + 1)
                        continue
                    if m >= 2:
                        dve.wait_ge(qz_done, 2 * (m - 1))
                        dve.wait_ge(qx_done, 2 * (m - 1))
                    if m < 4:
                        dve.tensor_tensor(qf[:, m % 2, :], rope_t[:, 0, :], rope_t[:, 1, :], ALU.add).then_inc(qf_ready, 1)
                        dve.wait_ge(qf_ready, m + 1)
                    else:
                        carry((kind, m), qf[:, m % 2, :], wide(T))
            for i in range(4):
                carry(("v", i, 1), V[:, 1, 256 * i:256 * i + 256], wide(256))
            for c, (a, r) in enumerate(CHUNKS):
                carry(("ko", c, 0), knat[0:r, c, 0:512], lambda ps: ps[0:r, :])

            def negate_max(s, views, at):
                settle()
                i = 0
                for v in views:
                    k = v.shape[1] if len(v.shape) == 3 else 1
                    step(dve.tensor_reduce(small[:, at + i:at + i + k], v, AX, ALU.max))
                    i += k
                settle()
                fronts[0] += 1
                dve.tensor_scalar(small[:, at + 4:at + 4 + i], small[:, at:at + i], -1.0, None, ALU.mult).then_inc(max_ready, 1)

            def divide(p, parts, at, sem_out):
                exps[0] += 1
                dve.wait_ge(exp_ready, exps[0])
                n = len(parts)
                step(dve.reciprocal(small[:, at + 12:at + 12 + n], small[:, at + 8:at + 8 + n]))
                settle()
                for i, (a, b) in enumerate(parts):
                    last = dve.tensor_scalar(p[:, a:b], p[:, a:b], small[:, at + 12 + i:at + 13 + i], None, ALU.mult)
                last.then_inc(sem_out, 1)

            def heads(t):
                return t.rearrange("p (h n) -> p h n", h=2)

            def pair_mask(name):
                return C(name).unsqueeze(1).broadcast_to([P, 2, P])

            def prompt_front(n):
                p = PAIR_ORDER[n]
                s = heads(tmp[0])
                ps = await_fill(dve, ("s0", p))[:, 0:256].rearrange("p (h n) -> p h n", h=2)
                dve.scalar_tensor_tensor(s[:, :, 0:P], ps, ATT_SCALE, pair_mask("causal"), ALU.mult, ALU.add).then_inc(read_sem(("s0", p)), 1)
                ps = heads(await_fill(dve, ("s1", p))[:, :])
                step(dve.tensor_scalar(s[:, :, P:256], ps[:, :, 0:P], ATT_SCALE, None, ALU.mult))
                dve.scalar_tensor_tensor(s[:, :, 256:384], ps[:, :, P:256], ATT_SCALE, pair_mask("causal"), ALU.mult, ALU.add).then_inc(read_sem(("s1", p)), 1)
                await_read(dve, ("s0", p))
                await_read(dve, ("s1", p))
                negate_max(tmp[0], [s[:, :, 0:P], s[:, :, P:384]], 0)

            PARTS = [(0, 128), (384, 512), (128, 384), (512, 768)]

            def suffix_sums(out, in_, ranges):
                for a, b in ranges:
                    src = in_[:, a:b][:, ::-1]
                    step(dve.tensor_tensor_scan(out[:, a:b][:, ::-1], src, C("zero").broadcast_to([P, b - a]), 0.0, ALU.add, ALU.add))

            def stick_middle(n, strict, strict_add, views, ranges):
                logs[0] += 1
                dve.wait_ge(log_ready, logs[0])
                z, l, sp, cum = tmp[2][:, 0:n], tmp[3][:, 0:n], tmp[4], tmp[5]
                step(dve.scalar_tensor_tensor(sp[:, 0:n], z, 0.0, l, ALU.max, ALU.add))
                settle()
                for v in views(sp):
                    step(dve.tensor_tensor(v, v, strict, ALU.mult))
                settle()
                suffix_sums(cum, sp, ranges)
                settle()
                step(dve.tensor_tensor(sp[:, 0:n], z, cum[:, 0:n], ALU.subtract))
                settle()
                for v in views(sp):
                    last = dve.tensor_tensor(v, v, strict_add, ALU.add)
                last.then_inc(arg_ready, 1)

            def prompt_stick(n):
                stick_middle(768, pair_mask("strict"), pair_mask("strict_add"),
                             lambda t: [heads(t)[:, :, 0:P], heads(t)[:, :, 256:384]],
                             [(0, 128), (128, 384), (384, 512), (512, 768)])

            prompt_front(0)
            prompt_stick(1)
            divide(tmp[1], PARTS, 0, prob_ready)
            dve.wait_ge(kv_stored, 16 * 4)
            for c in range(2):
                carry(("m", c, 0), memT[:, 0:4, P * c:P * c + P], by(4, P))
            for n, p in enumerate(PAIR_ORDER):
                if n >= 2:
                    await_fill(dve, ("o", PAIR_ORDER[n - 2]))
                carry(("t", p, 1), ptb[n % 2][1], wide(384))
                if n + 2 < NPAIR:
                    if n % 2 == 0:
                        prompt_front(n + 2)
                    else:
                        divide(tmp[1], PARTS, 0, prob_ready)
                        prompt_stick(n + 2)
                if n % 2 == 1:
                    carry(("mv", n // 2, 1), mvN[:, 1, 256 * (n // 2):256 * (n // 2) + 256], wide(256))
                carry(("o", p), aT[:, p, 0:NPT], wide(NPT))

            def keys_in(kind, b):
                if kind == "ck" and b >= 2:
                    dve.wait_ge(s_scored, b // 2)
                if kind == "mk":
                    dve.wait_ge(s_scored, 4 + b // 2)
                for j in (0, 2):
                    carry((kind, b, j), ktb[b % 2][:, 2 * j:2 * j + 2, 0:PAST], by(2, 256))

            def sample_front(quad):
                dve.wait_ge(s_scored, 2 * quad + 2)
                s = tmp[0]
                step(dve.tensor_scalar(s[:, 0:PAST], bank[4][:, 0:PAST], ATT_SCALE, None, ALU.mult))
                dve.scalar_tensor_tensor(s[:, PAST:T], bank[4][:, PAST:T], ATT_SCALE, C("new_causal", NS * quad, NS * quad + NS),
                                         ALU.mult, ALU.add).then_inc(scores_read[0], 1)
                dve.wait_ge(scores_read[0], quad + 1)
                negate_max(s, [s[:, 0:T]], 0)

            def sample_stick(quad):
                a, b = NS * quad, NS * quad + NS
                stick_middle(T, C("new_strict", a, b), C("new_strict_add", a, b), lambda t: [t[:, PAST:T]], [(0, T)])

            def sample_probs_in(quad):
                if quad == 0:
                    dve.wait_ge(zeroed, 8)
                    await_fill(dve, ("o", PAIR_ORDER[-1]))
                else:
                    dve.wait_ge(s_pv, 2)
                ps = await_fill(dve, ("st", quad, 1))
                copy(ptq[1][:, 0:2, :], ps[:, 0:256].rearrange("p (a b) -> p a b", b=P))
                copy(ptq[1][0:NS, 2, :], ps[0:NS, 256:384]).then_inc(read_sem(("st", quad, 1)), 1)

            def out_in(quad, f, n_pv, before):
                dve.wait_ge(s_pv, n_pv)
                if before is not None:
                    await_fill(dve, before)
                copy(so[1], bank[7][:, :]).then_inc(out_read[1], 1)

            keys_in("ck", 0)
            keys_in("ck", 1)
            keys_in("ck", 2)
            keys_in("ck", 3)
            sample_front(0)
            keys_in("ck", 4)
            sample_stick(0)
            keys_in("ck", 5)
            divide(tmp[1], [(0, T)], 0, s_prob)
            sample_probs_in(0)
            out_in(0, 1, 2, None)
            keys_in("ck", 6)
            keys_in("ck", 7)
            sample_front(1)
            place_sample_out(dve, copy, 0, 1)
            sample_stick(1)
            divide(tmp[1], [(0, T)], 0, s_prob)
            sample_probs_in(1)
            out_in(1, 1, 4, ("so", 0, 1))
            place_sample_out(dve, copy, 1, 1)

            for g in range(2):
                dve.wait_ge(rstd_ready, g + 1)
                if g == 0:
                    for quad in range(2):
                        await_read(dve, ("so", quad, 0))
                for m in range(4 * g, 4 * g + 4):
                    dve.scalar_tensor_tensor(aT[:, m, :], aT[:, m, :], vec[:, m:m + 1], rstd, ALU.mult, ALU.mult).then_inc(rms_done, 1)

            def add_residual(kind, n, x):
                for m in range(KB):
                    ps = await_fill(dve, (kind, m))
                    dve.scalar_tensor_tensor(yT[:, m, :], x[:, m, :], ALPHA, ps[:, 0:T], ALU.mult, ALU.add).then_inc(read_sem((kind, m)), 1)

            def layer_norm(n, gamma, mid):
                ps = await_fill(dve, ("mean", n))[:, 0:T].unsqueeze(1).broadcast_to([P, 4, T])
                for h in range(2):
                    y = yT[:, 4 * h:4 * h + 4, :]
                    last = dve.tensor_tensor(y, y, ps, ALU.subtract)
                    if h == 0:
                        last.then_inc(centered, 1)
                    else:
                        last.then_inc(read_sem(("mean", n)), 1)
                await_read(dve, ("mean", n))
                dve.sem_inc(centered, 1)
                mid()
                dve.wait_ge(rstd_ready, 2 + n + 1)
                dve.wait_ge(sq_ready, 2 + n + 1)
                for m in range(KB):
                    dve.scalar_tensor_tensor(yT[:, m, :], yT[:, m, :], vec[:, gamma + m:gamma + m + 1], rstd, ALU.mult, ALU.mult).then_inc(norm_mul, 1)

            for g in range(2):
                for h in range(2):
                    await_fill(dve, ("st", 1, g))
            dve.wait_ge(s_pv, 4)
            dve.wait_ge(kv_stored, 16 * 4)
            add_residual("y1", 0, xT)

            def mid():
                for m in (1, 3):
                    carry(("mk", m), mkT[:, m, :], wide(N_MEM))

            layer_norm(0, 8, mid)
            for m in (5, 7):
                carry(("mk", m), mkT[:, m, :], wide(N_MEM))
            for c in range(2):
                carry(("mko", c, 0), mknat[:, c, 0:512], wide(512))

            for m in range(0, KB, 2):
                carry(("mq", m), mqT[:, m, :], wide(T))

            def mem_front(h):
                s = tmp[2 * (h % 2)][:, 0:512]
                ps = await_fill(dve, ("ms", h))
                dve.tensor_scalar(s, ps[:, :], MEM_SCALE, None, ALU.mult).then_inc(read_sem(("ms", h)), 1)
                await_read(dve, ("ms", h))
                negate_max(s, [heads(s)], 16 * (h % 2))

            def mem_divide(h):
                divide(tmp[2 * (h % 2) + 1], [(0, 256), (256, 512)], 16 * (h % 2), prob_ready)

            mem_front(0)
            mem_front(1)
            keys_in("mk", 0)
            mem_divide(0)
            for h in range(4):
                if h + 1 < 4:
                    mem_divide(h + 1)
                if h + 2 < 4:
                    mem_front(h + 2)
                carry(("mo", h), oT[:, 2 * h:2 * h + 2, 0:NPT], by(2, 256))
            keys_in("mk", 1)

            def mem_sample_front(quad):
                dve.wait_ge(s_scored, 4 + 2 * quad + 2)
                s = tmp[6 + quad][:, 0:256]
                dve.tensor_scalar(s, bank[4 + quad][:, 0:256], MEM_SCALE, None, ALU.mult).then_inc(scores_read[0], 1)
                dve.wait_ge(scores_read[0], 2 + quad + 1)
                negate_max(s, [s], 16 * quad)

            keys_in("mk", 2)
            keys_in("mk", 3)
            keys_in("mk", 4)
            keys_in("mk", 5)
            mem_sample_front(0)
            keys_in("mk", 6)
            divide(tmp[6], [(0, 256)], 0, s_prob)
            keys_in("mk", 7)
            mem_sample_front(1)
            divide(tmp[7], [(0, 256)], 16, s_prob)
            out_in(0, 1, 6, ("so", 1, 1))
            place_mem_out(dve, copy, 0, 1)
            out_in(1, 1, 8, ("mso", 0, 1))
            place_mem_out(dve, copy, 1, 1)

            add_residual("y2", 1, x1T)

            def split_biases():
                dve.wait_ge(late_in, 16 * 8)
                for c in range(2):
                    a, b = 1024 * c, 1024 * c + 1024
                    settle()
                    step(copy(bgu_b[:, :], bgu_f[:, a:b]))
                    settle()
                    step(dve.tensor_tensor(bgu_r[:, a:b], bgu_f[:, a:b], bgu_b[:, :], ALU.subtract))
                    step(copy(bgu[0:32, a:b], bgu_b[0:32, :]))
                    settle()
                    step(copy(bgu_b[:, :], bgu_r[:, a:b]))
                    settle()
                    step(dve.tensor_tensor(bgu_r[:, a:b], bgu_r[:, a:b], bgu_b[:, :], ALU.subtract))
                    step(copy(bgu[32:64, a:b], bgu_b[32:64, :]))
                    settle()
                    step(copy(bgu[64:96, a:b], bgu_r[64:96, a:b]))

            layer_norm(1, 24, split_biases)

            ps = await_fill(dve, ("lg",))
            step(copy(logit[:, 0:2, :], ps[:, 0:64].rearrange("p (a b) -> p a b", b=NE)))
            copy(logit[0:NS, 2, :], ps[0:NS, 64:96]).then_inc(read_sem(("lg",)), 1)
            await_read(dve, ("lg",))
            settle()
            for c, (a, r) in enumerate(CHUNKS):
                step(dve.max(top[0:r, c, :], logit[0:r, c, :]))
            settle()
            for c, (a, r) in enumerate(CHUNKS):
                step(dve.max_index(topi[0:r, c, :], top[0:r, c, :], logit[0:r, c, :]))
                last = dve.tensor_scalar(small[0:r, c:c + 1], top[0:r, c, 0:1], -1.0, None, ALU.mult)
            last.then_inc(router_go, 1)
            settle()
            dve.wait_ge(zeroed, 13)
            step(copy(topf[:, 0:2, :], topi[:, 0:2, :]))
            step(copy(topf[0:NS, 2, :], topi[0:NS, 2, :]))
            dve.wait_ge(router_exp, 1)
            step(dve.reciprocal(small[:, 8:10], small[:, 4:6]))
            step(dve.reciprocal(small[0:NS, 10:11], small[0:NS, 6:7]))
            settle()
            for c, (a, r) in enumerate(CHUNKS):
                step(dve.tensor_scalar(gk[0:r, c, :], gk[0:r, c, :], small[0:r, 8 + c:9 + c], None, ALU.mult))
            experts = C("iota", 0, NE).unsqueeze(1).broadcast_to([P, TOPK, NE])
            for c in range(3):
                step(dve.tensor_tensor(eq[:, c], experts, topf[:, c, 0:TOPK].unsqueeze(2).broadcast_to([P, TOPK, NE]), ALU.is_equal))
            settle()
            step(dve.tensor_reduce(mask, eq.rearrange("p c k e -> p c e k"), AX, ALU.add))
            for c in range(3):
                step(dve.tensor_tensor(eqg[:, c], eq[:, c], gk[:, c, :].unsqueeze(2).broadcast_to([P, TOPK, NE]), ALU.mult))
            settle()
            dve.tensor_reduce(gates, eqg.rearrange("p c k e -> p c e k"), AX, ALU.add).then_inc(route_ready, 1)
            ps = await_fill(dve, ("rank",))
            step(dve.scalar_tensor_tensor(rankm, ps[:, 0:96].rearrange("p (a b) -> p a b", b=NE), 1.0, mask, ALU.add, ALU.mult))
            step(dve.tensor_scalar(nxf, ps[:, 96:128], float(CAP), None, ALU.is_gt))
            for k in range(2, 5):
                settle()
                if k < 4:
                    step(dve.scalar_tensor_tensor(nxf, ps[:, 96:128], float(CAP * k), nxf, ALU.is_gt, ALU.add))
                else:
                    dve.scalar_tensor_tensor(nxf, ps[:, 96:128], float(CAP * k), nxf, ALU.is_gt, ALU.add).then_inc(read_sem(("rank",)), 1)
            await_read(dve, ("rank",))
            step(dve.tensor_scalar(rankm, rankm, -1.0, None, ALU.add))
            step(copy(nextra, nxf))
            rest = [gate_s, sig_s]
            for i, (c, h) in enumerate([(c, h) for c in range(3) for h in range(2)]):
                r = CHUNKS[c][1]
                part = [tokn[0:r, s, c, 512 * h:512 * h + 512] for s in range(3)]
                a, t = acc[0:r, c, 512 * h:512 * h + 512], rest[i % 2][0:r, :]
                await_read(dve, ("tok", c, h))
                settle()
                step(copy(part[0], a))
                settle()
                step(dve.tensor_tensor(t, a, part[0], ALU.subtract))
                settle()
                step(copy(part[1], t))
                settle()
                step(dve.tensor_tensor(part[2], t, part[1], ALU.subtract))
                ps = await_fill(dve, ("bd", c, h))
                dve.scalar_tensor_tensor(a, a, ALPHA, ps[0:r, :], ALU.mult, ALU.add).then_inc(read_sem(("bd", c, h)), 1)
            for c in range(3):
                for h in range(2):
                    await_read(dve, ("bd", c, h))
            settle()
            dve.sem_inc(moe_ready, 1)

            dve.wait_ge(moe_ready, 3)
            dve.sem_inc(added, 1)
            blocks_done = dve.alloc_register("dve_blocks")
            dve.reg_mov(blocks_done, 0)
            COMB_BANK = (6, 7, 5, 4, 0)

            def add_outputs(n):
                dve.wait_ge(added, n * 5 + 1)
                for i in range(5):
                    dve.wait_ge(comb, n * 5 + i + 1)
                    c, h = divmod(i, 2)
                    a = acc[:, c, 512 * h:512 * h + 512] if i < 4 else acc2
                    ps = bank[COMB_BANK[i]][0:P if i < 4 else 64, :]
                    dve.tensor_tensor(a, a, ps, ALU.add).then_inc(added, 1)

            def expert_block():
                n = dve.snap(blocks_done)
                dve.wait_ge(gu_done, n + 1)
                dve.tensor_scalar(gate_s, bank[1][:, :], LIMIT, None, ALU.min).then_inc(sig_in, 1)
                dve.tensor_scalar(up_s, bank[2][:, :], LIMIT, -LIMIT, ALU.min, ALU.max).then_inc(moe_dve, 1)
                dve.wait_ge(moe_dve, n * 2 + 1)
                dve.wait_ge(sig_in, n + 1)
                dve.scalar_tensor_tensor(up_s, up_s, 1.0, gate_s, ALU.add, ALU.mult).then_inc(moe_dve, 1)
                dve.wait_ge(moe_dve, n * 2 + 2)
                dve.wait_ge(sig_ready, n + 1)
                dve.tensor_tensor(act_s, up_s, sig_s, ALU.mult).then_inc(act_ready, 1)
                add_outputs(n)
                dve.reg_add(blocks_done, blocks_done, 1)

            with dve.Fori(0, NE) as e:
                more = dve.value_load(nextra[0:1, bass.ds(e, 1)], min_val=0, max_val=4)
                with dve.If(more > 0):
                    with dve.Fori(0, more):
                        expert_block()
                expert_block()
            n = dve.snap(blocks_done)
            add_outputs(n)
            dve.wait_ge(added, n * 5 + 6)

            for h in range(2):
                step(copy(acc[0:NS, 2, 512 * h:512 * h + 512], acc2[32 * h:32 * h + 32, :]))
            stats = [gate_s, sig_s, up_s]
            settle()
            for c, (a, r) in enumerate(CHUNKS):
                st = stats[c][0:r, 0:12]
                for h in range(2):
                    step(dve.bn_stats(st[:, 6 * h:6 * h + 6], acc[0:r, c, 512 * h:512 * h + 512]))
                settle()
                dve.bn_aggr(small[0:r, 16 + 2 * c:18 + 2 * c], st).then_inc(fin_var, 1)
            for c, (a, r) in enumerate(CHUNKS):
                dve.wait_ge(fin_rstd, c + 1)
                dve.wait_ge(fin_var, c + 1)
                x = acc[0:r, c, :]
                step(dve.tensor_scalar(x, x, small[0:r, 16 + 2 * c:17 + 2 * c], small[0:r, 24 + c:25 + c], ALU.subtract, ALU.mult))
                settle()
                step(dve.tensor_tensor(x, x, ln3[0:r, 0, :], ALU.mult))
                settle()
                dve.tensor_tensor(x, x, ln3[0:r, 1, :], ALU.add).then_inc(fin_ready, 1)


_INS = ["x_prompt", "x_sample", "mem_prompt", "cache_k", "cache_v", "cache_mem_k", "cache_mem_v", "page_table",
        "w_in", "g_moba", "g_sb", "w_out", "ln1_g", "ln1_b", "w_mq", "w_mkv", "w_mo", "ln2_g", "ln2_b",
        "w_router", "b_router", "w_gu", "b_gu", "w_down", "b_down", "ln3_g", "ln3_b"]
_OUTS = [("y_prompt", (256, 1024), (1, 256, 1024)), ("y_sample", (32, 1024), (8, 4, 1024)),
         ("new_k_prompt", (256, 1024), (1, 1, 256, 16, 64)), ("new_v_prompt", (256, 1024), (1, 1, 256, 16, 64)),
         ("new_k_sample", (32, 1024), (1, 8, 4, 16, 64)), ("new_v_sample", (32, 1024), (1, 8, 4, 16, 64)),
         ("mem_k_prompt", (256, 1024), (1, 1, 256, 4, 256)), ("mem_v_prompt", (256, 1024), (1, 1, 256, 4, 256))]


def kernel(**inputs):
    import numpy as _np
    import concourse.bacc as _bacc
    from concourse.bass_utils import run_bass_kernel_spmd as _run

    nc = _bacc.Bacc("TRN2", target_bir_lowering=False, num_devices=1)
    arrays, ins, outs = {}, {}, {}
    for name in _INS:
        a = _np.ascontiguousarray(inputs[name])
        arrays[f"in_{name}"] = a
        ins[name] = nc.dram_tensor(f"in_{name}", a.shape, mybir.dt.from_np(a.dtype), kind="ExternalInput").ap()
    c = const_table()
    arrays["in_consts"] = c
    ins["consts"] = nc.dram_tensor("in_consts", c.shape, F32, kind="ExternalInput").ap()
    for name, shape, _ in _OUTS:
        outs[name] = nc.dram_tensor(f"out_{name}", shape, F32, kind="ExternalOutput").ap()
    build(nc, ins, outs)
    r = _run(nc, [arrays], core_ids=[0])
    return tuple(r.results[0][f"out_{name}"].reshape(shape) for name, _, shape in _OUTS)
```

```python
from contextlib import ExitStack

import concourse.bass as bass
from concourse import mybir

F32 = mybir.dt.float32
BF16 = mybir.dt.bfloat16
I32 = mybir.dt.int32
U32 = mybir.dt.uint32
ALU = mybir.AluOpType
ACT = mybir.ActivationFunctionType
AX = mybir.AxisListType.X

P = 128
D = 1024
KB = D // P
NPT = 256
NB_DEC, Q_DEC = 8, 4
NS = NB_DEC * Q_DEC
T = NPT + NS
CHUNKS = ((0, 128), (128, 128), (256, NS))
PAST = 256
PAGES = 2
N_PHYS = 20
HD = 64
NPAIR = 8
ATT_SCALE = HD ** -0.5
MEM_H = 4
MEM_SCALE = 256.0 ** -0.5
N_MEM = 256
ALPHA = 2.0 ** 0.25
LN_EPS, RMS_EPS = 1e-5, 1e-6
NE = 32
TOPK = 4
CAP = 64
LIMIT, SW_ALPHA = 7.0, 1.702
NEG = -1.0e30

CHUNKS_E = 12
RING = 12
ALL = 16
GROUP = 4
SLOT = 2048
LATE = 4
AREA = 25000
EARLY = 6
ROT = 4

CONST = {}
_at = 0
for _name, _n in (("ident", 128), ("rot", 128), ("cos", T), ("sin", T), ("causal", 128), ("strict", 128),
                  ("strict_add", 128), ("new_causal", 64), ("new_strict", 64), ("new_strict_add", 64),
                  ("tri", 128), ("one", 128), ("one1024", 128), ("one512", 128), ("slot2", 128), ("iota", 320), ("eye3", 32),
                  ("zero", 1), ("seat", 28)):
    CONST[_name] = (_at, _n)
    _at += _n
CONST_W = _at


def const_table():
    import numpy as np

    c = np.zeros((P, CONST_W), np.float32)

    def put(name, a):
        at, n = CONST[name]
        c[: a.shape[0], at:at + n] = a

    r = np.arange(P)
    put("ident", np.eye(P))
    rot = np.zeros((P, P))
    for m in range(P):
        if m % 64 < 32:
            rot[m + 32, m] = -1.0
        else:
            rot[m - 32, m] = 1.0
    put("rot", rot)
    half = HD // 2
    inv = (np.float32(10000.0) ** (-np.arange(half, dtype=np.float32) / np.float32(half))).astype(np.float32)
    pos = np.concatenate([np.arange(NPT), PAST + np.arange(NS) % Q_DEC]).astype(np.float32)
    ang = (pos[None, :] * inv[r % half][:, None]).astype(np.float32)
    put("cos", np.cos(ang.astype(np.float64)))
    put("sin", np.sin(ang.astype(np.float64)))
    put("causal", np.where(r[None, :] <= r[:, None], 0.0, NEG))
    put("strict", (r[None, :] < r[:, None]) * 1.0)
    put("strict_add", np.where(r[None, :] < r[:, None], 0.0, NEG))
    for quad in range(2):
        j = np.arange(NS)
        q = r % 4
        for name, g in (("new_causal", 0), ("new_strict", 1), ("new_strict_add", 1)):
            b = 4 * quad + (r // 32 - 2 * g) % 4
            same = (j[None, :] // 4) == b[:, None]
            ok = same & ((j[None, :] % 4 <= q[:, None]) if g == 0 else (j[None, :] % 4 < q[:, None]))
            at = CONST[name][0] + quad * NS
            c[:, at:at + NS] = ok if name == "new_strict" else np.where(ok, 0.0, NEG)
    put("tri", (r[:, None] < r[None, :]) * 1.0)
    put("one", np.ones((P, P)))
    put("one1024", np.full((P, P), 1 / 1024))
    put("one512", np.full((P, P), 1 / 512))
    put("slot2", np.tile(np.arange(CAP), 2)[None, :].repeat(P, 0))
    put("eye3", np.tile(np.eye(32), (3, 1)))
    first = [3, 11, 19, 7, 15, 0, 5, 9, 13]
    places = first + [i for i in range(NE - GROUP) if i not in first]
    put("seat", np.argsort(places)[None, :].repeat(P, 0))
    put("iota", np.arange(320)[None, :].repeat(P, 0))
    return c


def plan_items():
    items = [("xp",), ("xs",)]
    items += [("w", "k", i) for i in range(4)] + [("w", "q", i) for i in range(4)] + [("w", "v", i) for i in range(4)]
    items += [("mem",)] + [item for i in range(4) for item in (("w", "mv", i), ("ck", i))]
    items += [("ck", 4), ("ck", 5)] + [("cv", b) for b in range(4)]
    items += [("ck", 6), ("ck", 7), ("w", "mk", 0)] + [("cv", b) for b in range(4, 8)] + [("w", "mk", 1)]
    items += [("w", "o", i) for i in range(4)] + [("w", "mk", i) for i in (2, 3)]
    items += [("w", "mq", i) for i in range(4)]
    items += [("mk", b) for b in range(8)] + [("mv", b) for b in range(8)]
    items += [("w", "mo", i) for i in range(4)]
    return items


ITEMS = plan_items()
PAIR_ORDER = [0, 4, 1, 5, 2, 6, 3, 7]


def build(nc, A, O):
    ctx = ExitStack()
    with ctx:
        def sb(name, shape, dt=F32):
            return ctx.enter_context(nc.sbuf_tensor(name, shape, dt))

        def sem(name):
            return ctx.enter_context(nc.semaphore(name))

        ring = sb("ring", [P, RING * SLOT])
        consts = sb("consts", [P, CONST_W])
        area = sb("area", [P, AREA])
        pages = sb("pages", [1, NB_DEC * PAGES], I32)
        vec_rows = sb("vec_rows", [40, P])
        vec = sb("vec", [P, 40])
        small = sb("small", [P, 32])
        eps_small = sb("eps_small", [P, 3])
        bank = [ctx.enter_context(nc.psum_tensor(f"bank{i}", [P, 512], F32)) for i in range(8)]

        def C(name, a=0, b=None, rows=P):
            at, n = CONST[name]
            return consts[0:rows, at + a:at + (n if b is None else b)]

        def carve(base, at, *shape):
            n = 1
            for s in shape:
                n *= s
            v = base[:, at:at + n]
            if len(shape) == 2:
                v = v.rearrange("p (a b) -> p a b", a=shape[0])
            elif len(shape) == 3:
                v = v.rearrange("p (a b c) -> p a b c", a=shape[0], b=shape[1])
            return v

        def slot(i):
            return ring[:, i * SLOT:(i + 1) * SLOT]

        def chunk_slot(i):
            i %= ALL
            if i < RING:
                return slot(i)
            at = AREA - (ALL - i) * SLOT
            return area[:, at:at + SLOT]

        W0 = EARLY * SLOT
        xT = carve(ring, W0, KB, T)
        kT = carve(ring, W0 + 2304, NPAIR, T)
        x1T = kT
        mqT = carve(ring, W0 + 4608, KB, T)
        raw = carve(ring, W0 + 4608, 2, T)
        qf = carve(ring, W0 + 4608 + 576, 2, T)
        rope_t = carve(ring, W0 + 4608 + 1152, 2, T)
        aT = carve(ring, W0 + 6912, KB, T)
        oT = aT
        V = carve(ring, W0 + 9216, 3, D)
        yT = carve(ring, W0 + 9216, KB, T)
        x2T = yT

        ktb = [carve(area, i * 2304, NPAIR, T) for i in range(2)]
        sqT = carve(area, 0, KB, T)
        qx = carve(area, 4608, NB_DEC * NPAIR, 32)
        memT = carve(area, 6656, KB, N_MEM)
        mkT = carve(area, 8704, KB, N_MEM)
        mvN = carve(area, 10752, 2, D)
        knat = carve(area, 6656, 3, D)
        qz = carve(area, 12800, NPAIR * 2, NPT)
        mknat = carve(area, 12800, 2, D)
        tmp = [carve(area, 16896 + 768 * i, 768) for i in range(8)]
        so = [carve(area, 14848 + 512 * g, 512) for g in range(2)]
        lnv = area[:, 16212:16212 + T]
        rstd = area[:, 16500:16500 + T]
        ptb = [[carve(area, 23040 + 384 * (2 * i + hh), 384) for hh in range(2)] for i in range(2)]
        ptq = [carve(area, 23040 + 384 * g, 3, P) for g in range(2)]

        tokn = area[:, 0:4608].bitcast(BF16).rearrange("p (s c n) -> p s c n", s=3, c=3)
        acc = carve(area, 4608, 3, D)
        acc2 = area[0:64, 7680:8192]
        xgT = carve(area, 8192, KB, CAP)
        gate_s = carve(area, 8704, 512)
        sig_s = carve(area, 9216, 512)
        up_s = carve(area, 9728, 512)
        act_s = carve(area, 10240, 512)
        actT = carve(area, 10752, 4, P)
        y_s = carve(area, 11264, 512)
        token_rest = [gate_s, sig_s, up_s, act_s, area[:, 10752:11264], area[:, 8192:8704]]
        selT = [carve(area, 11776 + 288 * i, T) for i in range(2)]
        pick = area[:, 12352:12352 + 96].bitcast(BF16).rearrange("p (c n) -> p c n", c=3)
        gpick = carve(area, 12448, 3, P)
        rankm = carve(area, 12832, 3, NE)
        gates = carve(area, 12928, 3, NE)
        mask = carve(area, 13024, 3, NE)
        rcol = area[:, 13120:13123]
        gcol = area[:, 13124:13127]
        slots_now = area[:, 13128:13128 + 128]
        ebias = area[:, 13256:13256 + 32].bitcast(BF16)
        logT = area[:, 13288:13288 + T]
        logit = carve(area, 13576, 3, NE)
        top = carve(area, 13672, 3, 8)
        topi = area[:, 13696:13720].bitcast(U32).rearrange("p (c n) -> p c n", c=3)
        topf = carve(area, 13720, 3, 8)
        gk = carve(area, 13744, 3, TOPK)
        eq = carve(area, 13760, 3, TOPK, NE)
        eqg = carve(area, 14144, 3, TOPK, NE)
        tri16 = area[:, 14528:14592].bitcast(BF16)
        one16 = area[:, 14592:14656].bitcast(BF16)
        mask16 = area[:, 14656:14704].bitcast(BF16).rearrange("p (c n) -> p c n", c=3)
        nxf = area[:, 14816:14848]
        order = area[:, 14784:14816].bitcast(I32)
        nextra_at = area[:, 14848:14880].bitcast(I32)
        REST = NE - GROUP
        key, val = area[0:1, 16224:16224 + REST], area[0:1, 16256:16256 + REST]
        place = area[0:1, 16288:16288 + REST]
        cmp_s = carve(area, 13760, REST, REST)[0:1]
        who_s = carve(area, 10240, REST, REST)[0:1]
        nextra = area[:, 14880:14912].bitcast(I32)
        ebias_src = area[:, 14912:14928].bitcast(BF16)
        bgu = area[0:96, 14928:14928 + 1024].bitcast(BF16)
        w_router = carve(area, 15952, KB, NE)
        b_router = area[0:NE, 16208:16209]
        ln3 = carve(ring, 0, 2, D)
        bgu_f = area[0:96, 19968:19968 + 2048]
        bgu_r = area[0:96, 17024:17024 + 2048]

        const_in = sem("const_in")
        pages_in = sem("pages_in")
        vec_in = sem("vec_in")
        early_in = [sem(f"early_in{i}") for i in range(EARLY)]
        item_used = sem("item_used")
        slot_in = [sem(f"slot_in{i}") for i in range(ALL)]
        bias_split = sem("bias_split")
        ln3_in = sem("ln3_in")
        chunk_used = sem("chunk_used")
        gu_used = sem("gu_used")
        dn_used = sem("dn_used")
        bank_full = [sem(f"bank_full{i}") for i in range(ROT)]
        bank_read = [sem(f"bank_read{i}") for i in range(ROT)]
        dve_step = sem("dve_step")
        act_step = sem("act_step")
        pool_step = sem("pool_step")
        zeroed = sem("zeroed")
        eps_ready = sem("eps_ready")
        roped = sem("roped")
        stick_ready = sem("stick_ready")
        scores_read = [sem(f"scores_read{i}") for i in range(2)]
        out_read = [sem(f"out_read{i}") for i in range(2)]
        s_stick = sem("s_stick")
        centered = sem("centered")
        rms_done = sem("rms_done")
        moe_dve = sem("moe_dve")
        qf_ready = sem("qf_ready")
        qz_done = sem("qz_done")
        qx_done = sem("qx_done")
        new_keys = sem("new_keys")
        keys_stored = sem("keys_stored")
        values_stored = sem("values_stored")
        stored = sem("stored")
        prob_ready = sem("prob_ready")
        max_ready = sem("max_ready")
        exp_ready = sem("exp_ready")
        log_ready = sem("log_ready")
        arg_ready = sem("arg_ready")
        s_scored = sem("s_scored")
        s_prob = sem("s_prob")
        s_pv = sem("s_pv")
        sq_ready = sem("sq_ready")
        norm_mul = sem("norm_mul")
        norm_done = sem("norm_done")
        late_in = sem("late_in")
        bias_in = sem("bias_in")
        order_ready = sem("order_ready")
        mqx_done = sem("mqx_done")
        tables_in = sem("tables_in")
        router_exp = sem("router_exp")
        router_go = sem("router_go")
        token_high = sem("token_high")
        token_mid = sem("token_mid")
        tokens_ready = sem("tokens_ready")
        acc_ready = sem("acc_ready")
        route_ready = sem("route_ready")
        gates_ready = sem("gates_ready")
        gates_turned = sem("gates_turned")
        x2_used = sem("x2_used")
        moe_ready = sem("moe_ready")
        sel_ready = sem("sel_ready")
        picked = sem("picked")
        gates_picked = sem("gates_picked")
        xg_ready = sem("xg_ready")
        gu_done = sem("gu_done")
        sig_in = sem("sig_in")
        sig_ready = sem("sig_ready")
        act_ready = sem("act_ready")
        act_turned = sem("act_turned")
        actT_ready = sem("actT_ready")
        sel_turned = sem("sel_turned")
        selT_ready = sem("selT_ready")
        down_done = sem("down_done")
        y_ready = sem("y_ready")
        comb = sem("comb")
        added = sem("added")
        fin_var = sem("fin_var")
        fin_root = sem("fin_root")
        fin_scale = sem("fin_scale")
        fin_norm = sem("fin_norm")
        fin_pool = sem("fin_pool")
        y_stored = sem("y_stored")
        fin_ready = sem("fin_ready")

        fills = {}

        def use_of(name):
            return fills[name] % ROT, fills[name] // ROT

        def await_fill(eng, name):
            b, n = use_of(name)
            eng.wait_ge(bank_full[b], n + 1)
            return bank[b]

        def read_sem(name):
            return bank_read[use_of(name)[0]]

        def await_read(eng, name):
            b, n = use_of(name)
            eng.wait_ge(bank_read[b], n + 1)

        def await_query(eng, m):
            if m < 4:
                eng.wait_ge(qf_ready, m + 1)
            else:
                await_read(eng, ("q", m))

        def place_query(eng, copy, m):
            await_query(eng, m)
            for hh in range(2):
                copy(qz[HD * hh:HD * hh + HD, 2 * m + hh, :], qf[HD * hh:HD * hh + HD, m % 2, 0:NPT]).then_inc(qz_done, 1)

        def place_sample_out(eng, copy, quad, g):
            name = ("so", quad, g)
            ps = await_fill(eng, name)
            last = None
            for hh in range(2):
                rows = slice(HD * hh, HD * hh + HD)
                for r0, r1 in ((0, 4),) if g == 0 else ((0, 2), (2, 4)):
                    b0 = 4 * quad + (r0 - 2 * g) % 4
                    src = ps[rows, :].rearrange("p (j r i x) -> p j r i x", j=4, r=4, i=4)
                    for j in range(4):
                        last = copy(aT[rows, 4 * g + j, NPT + 4 * b0:NPT + 4 * (b0 + r1 - r0)].rearrange("p (r q) -> p r q", q=4),
                                    src[:, j, r0:r1, j, 4 * hh:4 * hh + 4])
            last.then_inc(read_sem(name), 1)

        def place_mem_out(eng, copy, quad, f):
            name = ("mso", quad, f)
            ps = await_fill(eng, name)
            src = ps[:, :].rearrange("p (k r x) -> p k r x", k=4, r=4)
            last = None
            for hl in range(2):
                h = 2 * f + hl
                for r0, r1 in ((0, 4),) if f == 0 else ((0, 2), (2, 4)):
                    b0 = 4 * quad + (r0 - 2 * f) % 4
                    for k in range(2):
                        last = copy(oT[:, 4 * f + 2 * hl + k, NPT + 4 * b0:NPT + 4 * (b0 + r1 - r0)].rearrange("p (r q) -> p r q", q=4),
                                    src[:, 2 * hl + k, r0:r1, 4 * h:4 * h + 4])
            last.then_inc(read_sem(name), 1)

        def third_part(eng, i):
            c, h = divmod(i, 2)
            r = CHUNKS[c][1]
            return eng.tensor_tensor(tokn[0:r, 2, c, 512 * h:512 * h + 512], token_rest[i][0:r, :],
                                     tokn[0:r, 1, c, 512 * h:512 * h + 512], ALU.subtract)

        def eps_col(eps, rows=P):
            i = 0 if eps == LN_EPS else 1
            return eps_small[0:rows, i:i + 1]

        slot_of, loads_of = {}, {}
        count = [0] * EARLY
        first = -len(ITEMS) % EARLY
        for i, item in enumerate(ITEMS):
            at = (first + i) % EARLY
            slot_of[item] = at
            count[at] += 32 if item[0] in ("ck", "cv") else 16
            loads_of[item] = count[at]

        def item_ap(item):
            s = slot(slot_of[item])
            if item[0] == "w":
                return s.rearrange("p (k n) -> p k n", k=KB)
            if item[0] == "xs":
                return s[0:NS, 0:D]
            return s.rearrange("p (c n) -> p c n", c=2)

        def w_view(ap, col):
            return ap[:, col:col + 256].rearrange("(k p) n -> p k n", p=P)

        win, wmkv = A["w_in"][0], A["w_mkv"][0]
        W_SRC = {
            "k": lambda i: w_view(win, 512 + 256 * i if i < 2 else 2048 + 256 * (i - 2)),
            "q": lambda i: w_view(win, 256 * i if i < 2 else 1536 + 256 * (i - 2)),
            "v": lambda i: w_view(win, 1024 + 256 * i if i < 2 else 2560 + 256 * (i - 2)),
            "mk": lambda i: w_view(wmkv, 256 * i),
            "mv": lambda i: w_view(wmkv, D + 256 * i),
            "o": lambda i: w_view(A["w_out"][0], 256 * i),
            "mq": lambda i: w_view(A["w_mq"][0], 256 * i),
            "mo": lambda i: w_view(A["w_mo"][0], 256 * i),
        }
        halves = lambda ap: ap.rearrange("(c p) n -> p c n", p=P)

        def gu_src(e, k):
            return A["w_gu"][0, bass.ds(e, 1), P * k:P * k + P, :].rearrange("a p n -> p (a n)")

        def dn_src(e, j):
            return A["w_down"][0, bass.ds(e, 1), 256 * j:256 * j + 256, :].rearrange("a (r p) n -> p (a r) n", p=P)

        block = ctx.enter_context(nc.Block())

        @block.tensor
        def _(pe):
            def open_fill(name):
                n = len(fills)
                fills[name] = n
                if n >= ROT:
                    pe.wait_ge(bank_read[n % ROT], n // ROT)
                return bank[n % ROT], bank_full[n % ROT]

            def arrived(item):
                pe.wait_ge(early_in[slot_of[item]], loads_of[item])
                return item_ap(item)

            def turn_blocks(name, pieces):
                ps, full = open_fill(name)
                at = 0
                for src in pieces:
                    rows, cols = src.shape[0], src.shape[1]
                    last = pe.transpose(ps[0:cols, at:at + rows], src, C("ident", 0, rows, rows))
                    at += rows
                return last, full

            def project_T(name, w, col, src, n, blocks=None):
                ps, full = open_fill(name)
                for k in range(KB):
                    if blocks is not None:
                        pe.wait_ge(blocks[0], blocks[1] + k + 1)
                    last = pe.matmul(ps[:, 0:n], w[:, k, col:col + P], src[:, k, 0:n], start=(k == 0), stop=(k == KB - 1))
                last.then_inc(full, 1)
                return last

            def project_N(name, w, src, c):
                a, r = CHUNKS[c]
                ps, full = open_fill(name)
                for k in range(KB):
                    last = pe.matmul(ps[0:r, 0:256], src[:, k, a:a + r], w[:, k, :], start=(k == 0), stop=(k == KB - 1))
                last.then_inc(full, 1)
                return last

            def used():
                pe.wait_ge(*last_fill())
                pe.sem_inc(item_used, 1)

            def last_fill():
                n = len(fills) - 1
                return bank_full[n % ROT], n // ROT + 1

            pe.wait_ge(const_in, 16)
            x = arrived(("xp",))
            for c in range(2):
                for j in range(2):
                    last, full = turn_blocks(("x", c, j), [x[:, c, P * b:P * b + P] for b in range(4 * j, 4 * j + 4)])
                    last.then_inc(full, 1)
            used()
            x = arrived(("xs",))
            last, full = turn_blocks(("x", 2, 0), [x[:, P * b:P * b + P] for b in range(KB)])
            last.then_inc(full, 1)
            used()
            for name in (("x", 0, 0), ("x", 0, 1), ("x", 1, 0), ("x", 1, 1), ("x", 2, 0)):
                await_read(pe, name)

            def rotate(kind, m):
                await_read(pe, (kind, m))
                if kind == "k" and m == 0:
                    pe.wait_ge(const_in, 32)
                ps, full = open_fill((kind + "r", m))
                pe.matmul(ps[:, 0:T], C("rot"), raw[:, m % 2, :], start=True, stop=True).then_inc(full, 1)

            for kind in "kq":
                for i in range(4):
                    w = arrived(("w", kind, i))
                    for h in range(2):
                        m = 2 * i + h
                        project_T((kind, m), w, P * h, xT, T)
                        if h == 1:
                            used()
                        if 1 <= m <= 4:
                            rotate(kind, m - 1)
            for m in range(4, 8):
                await_read(pe, ("k", m))
            pe.wait_ge(roped, 4)
            for c, (a, r) in enumerate(CHUNKS):
                for j in range(2):
                    last, full = turn_blocks(("ko", c, j), [kT[:, b, a:a + r] for b in range(4 * j, 4 * j + 4)])
                    last.then_inc(full, 1)

            def score(p):
                ps, full = open_fill(("s0", p))
                for hh in range(2):
                    last = pe.matmul(ps[:, P * hh:P * hh + P], qz[:, 2 * p + hh, 0:P], kT[:, p, 0:P], start=True, stop=True)
                last.then_inc(full, 1)
                ps, full = open_fill(("s1", p))
                for hh in range(2):
                    last = pe.matmul(ps[:, 256 * hh:256 * hh + 256], qz[:, 2 * p + hh, P:256], kT[:, p, 0:256], start=True, stop=True)
                last.then_inc(full, 1)

            def turn_probs(n, p):
                pe.wait_ge(prob_ready if p < 4 else stick_ready, n // 2 + 1)
                src = tmp[1] if p < 4 else tmp[6]
                for hh in range(2):
                    last, full = turn_blocks(("t", p, hh), [src[:, 384 * hh + P * j:384 * hh + P * j + P] for j in range(3)])
                    last.then_inc(full, 1)

            def attend(n, p):
                await_read(pe, ("t", p, 0))
                await_read(pe, ("t", p, 1))
                ps, full = open_fill(("o", p))
                for kc in range(2):
                    for hh in range(2):
                        pt = ptb[n % 2][hh]
                        v = V[:, kc, P * p + HD * hh:P * p + HD * hh + HD]
                        if kc == 0:
                            last = pe.matmul(ps[HD * hh:HD * hh + HD, 0:256], v, pt[:, 0:256], start=True, stop=False)
                        else:
                            last = pe.matmul(ps[HD * hh:HD * hh + HD, P:256], v, pt[:, 256:384], start=False, stop=True)
                last.then_inc(full, 1)

            for i in range(4):
                w = arrived(("w", "v", i))
                for c in range(2):
                    project_N(("v", i, c), w, xT, c)
                if i == 1:
                    pe.wait_ge(qz_done, 2 * NPAIR)
                    score(PAIR_ORDER[0])
                    score(PAIR_ORDER[1])
            ps, full = open_fill(("vs",))
            for k in range(KB):
                for i in range(4):
                    last = pe.matmul(ps[NS * i:NS * i + NS, 0:256], xT[:, k, NPT:T], item_ap(("w", "v", i))[:, k, :],
                                     start=(k == 0), stop=(k == KB - 1))
            last.then_inc(full, 1)
            pe.wait_ge(*last_fill())
            pe.sem_inc(item_used, 4)
            pe.wait_ge(vec_in, 16 * 6)
            last, full = turn_blocks(("vec",), [vec_rows[:, :]])
            last.then_inc(full, 1)
            x = arrived(("mem",))
            for c in range(2):
                for j in range(2):
                    last, full = turn_blocks(("m", c, j), [x[:, c, P * b:P * b + P] for b in range(4 * j, 4 * j + 4)])
                    last.then_inc(full, 1)
            used()
            S_BANK, O_BANK = (4, 5), (6, 7)

            def turn_keys(b, kind="ck"):
                x = arrived((kind, b))
                for j in range(4):
                    last, full = turn_blocks((kind, b, j), [x[:, c, P * q:P * q + P] for q in (2 * j, 2 * j + 1) for c in range(2)])
                    last.then_inc(full, 1)
                used()

            def score_pair(b0):
                for b in (b0, b0 + 1):
                    for j in range(4):
                        await_read(pe, ("ck", b, j))
                if b0 == 0:
                    pe.wait_ge(new_keys, 2)
                    pe.wait_ge(qx_done, 2 * NPAIR)
                if b0 == 4:
                    for g in range(2):
                        pe.wait_ge(scores_read[g], 1)
                for j in range(4):
                    for g in range(2):
                        for b in (b0, b0 + 1):
                            r = (b + 2 * g) % 4
                            last = pe.matmul(bank[S_BANK[g]][32 * r:32 * r + 32, 0:T], qx[:, b * NPAIR + 4 * g + j, :],
                                             ktb[b % 2][:, 4 * g + j, :], start=(j == 0), stop=(j == 3))
                last.then_inc(s_scored, 1)

            def turn_sample_probs(quad):
                for g in range(2):
                    pe.wait_ge(s_stick if g else s_prob, quad + 1)
                    src = tmp[1] if g == 0 else tmp[6]
                    last, full = turn_blocks(("st", quad, g), [src[:, 0:P], src[:, P:256], src[:, 256:288]])
                    last.then_inc(full, 1)

            def attend_pair(b0):
                quad = b0 // 4
                if b0 % 4 == 0:
                    for g in range(2):
                        await_read(pe, ("st", quad, g))
                    if quad:
                        for g in range(2):
                            pe.wait_ge(out_read[g], 1)
                vs = [arrived(("cv", b)) for b in (b0, b0 + 1)]
                for kk in range(3):
                    for g in range(2):
                        for b in (b0, b0 + 1):
                            r = (b + 2 * g) % 4
                            v = vs[b - b0][:, kk, 512 * g:512 * g + 512] if kk < 2 else V[:, 2, 512 * g:512 * g + 512]
                            last = pe.matmul(bank[O_BANK[g]][32 * r:32 * r + 32, :], ptq[g][:, kk, 32 * r:32 * r + 32], v,
                                             start=(kk == 0), stop=(kk == 2))
                last.then_inc(s_pv, 1)
                pe.wait_ge(s_pv, b0 // 2 + 1)
                pe.sem_inc(item_used, 2)

            def turn_sample_out(quad):
                for g in range(2):
                    pe.wait_ge(out_read[g], quad + 1)
                    src = so[g]
                    last, full = turn_blocks(("so", quad, g), [src[:, P * j:P * j + P] for j in range(4)])
                    last.then_inc(full, 1)

            for c in range(2):
                for j in range(2):
                    await_read(pe, ("m", c, j))
            for i in range(4):
                for c in range(2):
                    await_read(pe, ("v", i, c))
            await_read(pe, ("vs",))
            for n, p in enumerate(PAIR_ORDER):
                turn_probs(n, p)
                if n + 2 < NPAIR:
                    score(PAIR_ORDER[n + 2])
                if n % 2 == 0:
                    w = arrived(("w", "mv", n // 2))
                    project_N(("mv", n // 2, 0), w, memT, 0)
                    attend(n, p)
                    project_N(("mv", n // 2, 1), w, memT, 1)
                    used()
                else:
                    if n == 5:
                        score_pair(0)
                    turn_keys(n // 2)
                    attend(n, p)

            score_pair(2)
            def project_mem_keys(m):
                w = arrived(("w", "mk", m // 2))
                project_T(("mk", m), w, P * (m % 2), memT, N_MEM)
                if m % 2:
                    used()

            turn_keys(4)
            turn_keys(5)
            turn_sample_probs(0)
            score_pair(4)
            attend_pair(0)
            attend_pair(2)
            turn_keys(6)
            turn_keys(7)
            score_pair(6)
            project_mem_keys(0)
            project_mem_keys(1)
            turn_sample_out(0)
            turn_sample_probs(1)
            attend_pair(4)
            attend_pair(6)
            turn_sample_out(1)

            project_mem_keys(2)
            for g in range(2):
                pe.wait_ge(sq_ready, g + 1)
                ps, full = open_fill(("rms", g))
                for j in range(4):
                    last = pe.matmul(ps[:, 0:T], C("one512"), sqT[:, 4 * g + j, :], start=(j == 0), stop=(j == 3))
                last.then_inc(full, 1)

            project_mem_keys(3)

            def mean_fill(n, kind):
                ps, full = open_fill(("mean", n))
                for m in range(KB):
                    await_read(pe, (kind, m))
                    last = pe.matmul(ps[:, 0:T], C("one1024"), yT[:, m, :], start=(m == 0), stop=(m == KB - 1))
                last.then_inc(full, 1)

            def var_fill(n):
                ps, full = open_fill(("var", n))
                for m in range(KB):
                    if m % 2 == 0:
                        pe.wait_ge(sq_ready, 2 + 4 * n + m // 2 + 1)
                    last = pe.matmul(ps[:, 0:T], C("one1024"), sqT[:, m, :], start=(m == 0), stop=(m == KB - 1))
                last.then_inc(full, 1)

            for i in range(4):
                w = arrived(("w", "o", i))
                for h in range(2):
                    project_T(("y1", 2 * i + h), w, P * h, aT, T, (rms_done, 0) if i + h == 0 else None)
                used()
            mean_fill(0, "y1")
            project_mem_keys(4)
            project_mem_keys(5)
            var_fill(0)
            project_mem_keys(6)
            project_mem_keys(7)
            for i in range(4):
                w = arrived(("w", "mq", i))
                for h in range(2):
                    project_T(("mq", 2 * i + h), w, P * h, x1T, T, (norm_done, 0) if i + h == 0 else None)
                used()
            for m in range(KB):
                await_read(pe, ("mk", m))
            for m in range(KB):
                await_read(pe, ("mq", m))

            def mem_score(h):
                ps, full = open_fill(("ms", h))
                for c in range(2):
                    for f in range(2):
                        last = pe.matmul(ps[:, 256 * c:256 * c + 256], mqT[:, 2 * h + f, P * c:P * c + P],
                                         mkT[:, 2 * h + f, :], start=(f == 0), stop=(f == 1))
                last.then_inc(full, 1)

            def mem_turn(h):
                pe.wait_ge(prob_ready, 4 + h + 1)
                src = tmp[2 * (h % 2) + 1]
                last, full = turn_blocks(("mp", h), [src[:, 256 * c + P * kc:256 * c + P * kc + P] for kc in range(2) for c in range(2)])
                last.then_inc(full, 1)

            def mem_attend(h):
                await_read(pe, ("mp", h))
                ps, full = open_fill(("mo", h))
                for f in range(2):
                    for kc in range(2):
                        last = pe.matmul(ps[:, 256 * f:256 * f + 256], mvN[:, kc, 256 * h + P * f:256 * h + P * f + P],
                                         tmp[4 + h % 2][:, 256 * kc:256 * kc + 256], start=(kc == 0), stop=(kc == 1))
                last.then_inc(full, 1)

            def mem_score_pair(b0):
                for b in (b0, b0 + 1):
                    for j in range(4):
                        await_read(pe, ("mk", b, j))
                if b0 == 0:
                    pe.wait_ge(mqx_done, 1)
                for m in range(KB):
                    for b in (b0, b0 + 1):
                        r = b % 4
                        last = pe.matmul(bank[S_BANK[b // 4]][32 * r:32 * r + 32, 0:N_MEM], qx[:, b * KB + m, :],
                                         ktb[b % 2][:, m, 0:N_MEM], start=(m == 0), stop=(m == KB - 1))
                last.then_inc(s_scored, 1)

            def mem_turn_sample(quad):
                pe.wait_ge(s_prob, 2 + quad + 1)
                src = tmp[6 + quad]
                last, full = turn_blocks(("mst", quad), [src[:, 0:P], src[:, P:256]])
                last.then_inc(full, 1)

            def mem_attend_pair(b0):
                quad = b0 // 4
                if b0 % 4 == 0:
                    await_read(pe, ("mst", quad))
                    for f in range(2):
                        pe.wait_ge(out_read[f], 2 + quad)
                vs = [arrived(("mv", b)) for b in (b0, b0 + 1)]
                for kk in range(2):
                    for f in range(2):
                        for b in (b0, b0 + 1):
                            r, rp = (b + 2 * f) % 4, b % 4
                            last = pe.matmul(bank[O_BANK[f]][32 * r:32 * r + 32, :], ptq[quad][:, kk, 32 * rp:32 * rp + 32],
                                             vs[b - b0][:, kk, 512 * f:512 * f + 512], start=(kk == 0), stop=(kk == 1))
                last.then_inc(s_pv, 1)
                pe.wait_ge(s_pv, 4 + b0 // 2 + 1)
                pe.sem_inc(item_used, 2)

            def mem_turn_out(quad):
                for f in range(2):
                    pe.wait_ge(out_read[f], 2 + quad + 1)
                    last, full = turn_blocks(("mso", quad, f), [so[f][:, P * j:P * j + P] for j in range(4)])
                    last.then_inc(full, 1)

            def turn_mem_keys_back(c):
                for j in range(2):
                    last, full = turn_blocks(("mko", c, j), [mkT[:, b, P * c:P * c + P] for b in range(4 * j, 4 * j + 4)])
                    last.then_inc(full, 1)

            mem_score(0)
            mem_score(1)
            turn_keys(0, "mk")
            for h in range(4):
                mem_turn(h)
                if h + 2 < 4:
                    mem_score(h + 2)
                mem_attend(h)
            turn_keys(1, "mk")
            mem_score_pair(0)
            for b0 in (2, 4, 6):
                turn_keys(b0, "mk")
                turn_keys(b0 + 1, "mk")
                mem_score_pair(b0)
            mem_turn_sample(0)
            mem_attend_pair(0)
            mem_attend_pair(2)
            mem_turn_sample(1)
            mem_turn_out(0)
            turn_mem_keys_back(0)
            mem_attend_pair(4)
            mem_attend_pair(6)
            turn_mem_keys_back(1)
            mem_turn_out(1)

            for h in range(4):
                await_read(pe, ("mo", h))
            for quad in range(2):
                for f in range(2):
                    await_read(pe, ("mso", quad, f))
            for i in range(4):
                w = arrived(("w", "mo", i))
                for h in range(2):
                    project_T(("y2", 2 * i + h), w, P * h, oT, T)
                used()
            mean_fill(1, "y2")
            var_fill(1)
            def turn_tokens(c, h):
                a, r = CHUNKS[c]
                last, full = turn_blocks(("tok", c, h), [x2T[:, b, a:a + r] for b in range(4 * h, 4 * h + 4)])
                last.then_inc(full, 1)

            pe.wait_ge(late_in, 16 * LATE)
            ps, full = open_fill(("lgT",))
            for k in range(KB):
                pe.wait_ge(norm_done, KB + k + 1)
                last = pe.matmul(ps[0:NE, 0:T], w_router[:, k, :], x2T[:, k, :], start=(k == 0), stop=(k == KB - 1))
            last.then_inc(full, 1)
            turn_tokens(0, 0)
            turn_tokens(0, 1)
            await_read(pe, ("lgT",))
            ps, full = open_fill(("lg",))
            for c, (a, r) in enumerate(CHUNKS):
                last = pe.transpose(ps[0:r, NE * c:NE * c + NE], logT[0:NE, a:a + r], C("ident", 0, NE, NE))
            last.then_inc(full, 1)
            for c in (1, 2):
                for h in range(2):
                    turn_tokens(c, h)
            pe.wait_ge(*last_fill())
            pe.sem_inc(x2_used, 1)
            pe.sem_inc(picked, 1)
            pe.sem_inc(sel_turned, 1)
            pe.wait_ge(zeroed, 16)
            pe.wait_ge(route_ready, 1)
            ps, full = open_fill(("rank",))
            for c in range(3):
                for d in range(c + 1):
                    pe.matmul(ps[:, NE * c:NE * c + NE], tri16 if d == c else one16, mask16[:, d, :], start=(d == 0), stop=(d == c))
            for d in range(3):
                last = pe.matmul(ps[:, 96:128], one16, mask16[:, d, :], start=(d == 0), stop=(d == 2))
            last.then_inc(full, 1)
            for c in range(3):
                for h in range(2):
                    await_read(pe, ("tok", c, h))
            for name in (("lg",), ("rank",)):
                await_read(pe, name)
            pe.wait_ge(moe_ready, 1)
            pe.wait_ge(tokens_ready, 4)
            pe.wait_ge(route_ready, 2)

            blocks_done = pe.alloc_register("pe_blocks")
            pe.reg_mov(blocks_done, 0)
            COMB_BANK = (5, 0, 4, 6, 7)

            def combine():
                for c in range(2):
                    for h in range(2):
                        pe.matmul(bank[COMB_BANK[2 * c + h]][:, :], selT[h][:, P * c:P * c + P], y_s[:, :],
                                  start=True, stop=True).then_inc(comb, 1)
                for h in range(2):
                    last = pe.matmul(bank[COMB_BANK[4]][32 * h:32 * h + 32, :], selT[h][:, 256:T], y_s[:, :], start=True, stop=True)
                last.then_inc(comb, 1)

            def gather(n):
                pe.wait_ge(sel_ready, n + 1)
                for m in range(KB):
                    for c in range(3):
                        for part in range(3):
                            last = pe.matmul(bank[0][:, CAP * m:CAP * m + CAP], tokn[:, part, c, P * m:P * m + P], pick[:, c, :],
                                             start=(c == 0 and part == 0), stop=(c == 2 and part == 2))
                last.then_inc(picked, 1)

            gather(0)
            pe.wait_ge(gates_ready, 1)
            for c, (a, r) in enumerate(CHUNKS):
                last = pe.transpose(bank[5][0:NE, a:a + r], gates[0:r, c, :], C("ident", 0, r, r))
            last.then_inc(gates_turned, 1)

            def chunk_arrived(group, q, j):
                i = CHUNKS_E * q + j
                turns = GROUP * CHUNKS_E // ALL
                pe.wait_ge(slot_in[i % ALL], group * (16 * turns) + 16 * (i // ALL + 1))
                return chunk_slot(i)

            def expert_block(group, q, release, last_block=False):
                n = pe.snap(blocks_done)
                pe.wait_ge(gates_picked, n + 1)
                for j in range(2):
                    for h in range(2):
                        pe.matmul(bank[1 + j][64 * h:64 * h + 64, :], ebias[0:96, :], bgu[:, D * j + 512 * h:D * j + 512 * h + 512],
                                  start=True, stop=False)
                pe.wait_ge(xg_ready, n + 1)
                for k in range(KB):
                    w = chunk_arrived(group, q, k)
                    for j in range(2):
                        for h in range(2):
                            last = pe.matmul(bank[1 + j][64 * h:64 * h + 64, :], xgT[:, k, :], w[:, D * j + 512 * h:D * j + 512 * h + 512],
                                             start=False, stop=(k == KB - 1))
                    if release and k < KB - 1:
                        last.then_inc(chunk_used, 1)
                last.then_inc(gu_done, 1)
                pe.wait_ge(y_ready, n + 1)
                pe.wait_ge(selT_ready, n + 1)
                pe.wait_ge(added, n * 5 + 1)
                combine()
                pe.wait_ge(act_ready, n + 1)
                for j in range(4):
                    last = pe.transpose(bank[3][:, P * j:P * j + P], act_s[:, P * j:P * j + P], C("ident"))
                last.then_inc(act_turned, 1)
                pe.wait_ge(added, n * 5 + 2)
                for c, (a, r) in enumerate(CHUNKS):
                    last = pe.transpose(bank[5][:, a:a + r], gpick[0:r, c, :], C("ident", 0, r, r))
                last.then_inc(sel_turned, 1)
                if not last_block:
                    pe.wait_ge(added, n * 5 + 3)
                    gather(n + 1)
                pe.wait_ge(added, n * 5 + 4)
                pe.wait_ge(actT_ready, n + 1)
                for i in range(4):
                    w = chunk_arrived(group, q, KB + i).rearrange("p (r n) -> p r n", r=2)
                    for r in range(2):
                        f = 2 * i + r
                        for h in range(2):
                            last = pe.matmul(bank[4][64 * h:64 * h + 64, :], actT[:, f % 4, 64 * (f // 4):64 * (f // 4) + 64],
                                             w[:, r, 512 * h:512 * h + 512], start=(f == 0), stop=(f == KB - 1))
                    if release and i < 3:
                        last.then_inc(chunk_used, 1)
                last.then_inc(down_done, 1)
                pe.reg_add(blocks_done, blocks_done, 1)

            def further_blocks(group, q, counts):
                more = pe.value_load(counts[0:1, bass.ds(group * GROUP + q, 1)], min_val=0, max_val=4)
                with pe.If(more > 0):
                    with pe.Fori(0, more):
                        expert_block(group, q, False)

            for q in range(GROUP):
                further_blocks(0, q, nextra)
                expert_block(0, q, True)
            pe.wait_ge(order_ready, 1)
            last_group = NE // GROUP - 1
            with pe.Fori(1, last_group) as group:
                for q in range(GROUP):
                    further_blocks(group, q, nextra_at)
                    expert_block(group, q, True)
            for q in range(GROUP):
                further_blocks(last_group, q, nextra_at)
                expert_block(last_group, q, True, last_block=(q == GROUP - 1))
            n = pe.snap(blocks_done)
            pe.wait_ge(y_ready, n + 1)
            pe.wait_ge(selT_ready, n + 1)
            pe.wait_ge(added, n * 5 + 1)
            combine()

        @block.sync
        def _(sp):
            sp.dma_start(C("ident"), A["consts"][:, 0:P]).then_inc(const_in, 16)
            sp.dma_start(pages[0:1, :], A["page_table"].rearrange("(a b) g -> a (b g)", a=1)).then_inc(pages_in, 16)

            def early(i):
                item = ITEMS[i]
                if i >= EARLY:
                    sp.wait_ge(item_used, i - EARLY + 1)
                dst, s = item_ap(item), early_in[slot_of[item]]
                if item[0] == "xp":
                    sp.dma_start(dst, halves(A["x_prompt"][0])).then_inc(s, 16)
                elif item[0] == "xs":
                    sp.dma_start(dst, A["x_sample"].rearrange("b q n -> (b q) n")).then_inc(s, 16)
                elif item[0] == "mem":
                    sp.dma_start(dst, halves(A["mem_prompt"][0])).then_inc(s, 16)
                elif item[0] == "w":
                    sp.dma_start(dst, W_SRC[item[1]](item[2])).then_inc(s, 16)
                elif item[0] in ("ck", "cv"):
                    src = A["cache_k" if item[0] == "ck" else "cache_v"]
                    if item == ("ck", 0):
                        sp.wait_ge(pages_in, 16)
                    for g in range(PAGES):
                        at = item[1] * PAGES + g
                        page = sp.value_load(pages[0:1, at:at + 1], min_val=0, max_val=N_PHYS - 1)
                        sp.dma_start(dst[:, g, :], src[0, bass.ds(page, 1)].rearrange("a t h d -> t (a h d)")).then_inc(s, 16)
                else:
                    src = A["cache_mem_k" if item[0] == "mk" else "cache_mem_v"]
                    sp.dma_start(dst, src[0, item[1]].rearrange("(c p) h d -> p c (h d)", p=P)).then_inc(s, 16)

            for i in range(len(ITEMS)):
                early(i)
                if i == 2:
                    sp.dma_start(consts[:, P:], A["consts"][:, P:]).then_inc(const_in, 16)

            def chunk(e, i):
                j = i % CHUNKS_E
                dst, s = chunk_slot(i), slot_in[i % ALL]
                if j < KB:
                    sp.dma_start(dst, gu_src(e, j)).then_inc(s, 16)
                else:
                    sp.dma_start(dst.rearrange("p (r n) -> p r n", r=2), dn_src(e, j - KB)).then_inc(s, 16)

            for m in range(KB):
                await_read(sp, ("y1", m))
            chunk(0, EARLY)
            for i in range(EARLY):
                sp.wait_ge(item_used, len(ITEMS) - EARLY + i + 1)
                chunk(0, i)
            for m in range(KB):
                await_read(sp, ("y2", m))
            sp.wait_ge(mqx_done, 1)
            for i in range(EARLY + 1, EARLY + 4):
                chunk(0, i)
            sp.wait_ge(bias_split, 1)
            for i in range(RING, ALL):
                chunk(1, i)
            sp.wait_ge(x2_used, 1)
            for i in range(EARLY + 4, RING):
                chunk(0, i)

            def slot_free(e, j):
                if j == KB - 1:
                    sp.wait_ge(gu_used, e + 1)
                elif j == CHUNKS_E - 1:
                    sp.wait_ge(dn_used, e + 1)
                else:
                    sp.wait_ge(chunk_used, e * (CHUNKS_E - 2) + (j + 1 if j < KB else j))

            for i in range(ALL, GROUP * CHUNKS_E):
                slot_free(*divmod(i - ALL, CHUNKS_E))
                chunk(i // CHUNKS_E, i)
            sp.wait_ge(order_ready, 1)
            with sp.Fori(1, NE // GROUP) as group:
                for i in range(GROUP * CHUNKS_E):
                    if i % CHUNKS_E == 0:
                        e = sp.value_load(order[0:1, bass.ds(group * GROUP + i // CHUNKS_E, 1)], min_val=0, max_val=NE - 1)
                    before, j = divmod(i - ALL, CHUNKS_E)
                    slot_free(group * GROUP + before, j)
                    chunk(e, i)
            for j in range(KB, CHUNKS_E):
                slot_free(NE - 2, j)
            for i, name in enumerate(("ln3_g", "ln3_b")):
                sp.dma_start(ln3[:, i, :], A[name].broadcast_to([P, D])).then_inc(ln3_in, 16)

            sp.wait_ge(fin_pool, 2)
            sp.dma_start(O["y_prompt"][0:P, :], acc[:, 0, :]).then_inc(y_stored, 16)
            sp.wait_ge(fin_ready, 1)
            sp.wait_ge(fin_pool, 4)
            sp.dma_start(O["y_prompt"][P:NPT, :], acc[:, 1, :]).then_inc(y_stored, 16)
            sp.wait_ge(y_stored, 16 * 3)

        @block.gpsimd
        def _(pool):
            done = [0]

            def step(ins):
                done[0] += 1
                ins.then_inc(pool_step, 1)

            def settle():
                pool.wait_ge(pool_step, done[0])

            rows = [("g_moba", 0, 4), ("g_sb", 4, 4), ("ln1_g", 8, 8), ("ln1_b", 16, 8), ("ln2_g", 24, 8), ("ln2_b", 32, 8)]
            for name, at, n in rows:
                pool.dma_start(vec_rows[at:at + n, :], A[name][0].rearrange("(a p) -> a p", p=P)).then_inc(vec_in, 16)
            cleared = [0]

            def clear(view, value=0.0):
                pool.memset(view, value).then_inc(zeroed, 1)
                cleared[0] += 1
                pool.wait_ge(zeroed, cleared[0])

            clear(qz)
            clear(qx)
            clear(V[32:64, 2, :])
            clear(V[64:128, 2, :])

            def spread(src, m, sem_out):
                for hh in range(2):
                    at = (m % 4) * 8 + hh * 4
                    if m or hh:
                        pool.wait_ge(sem_out, 2 * m + hh)
                    out = qx[HD * hh:HD * hh + HD, :, at:at + 4].rearrange("p (b g) q -> p b g q", b=NB_DEC)[:, :, m, :]
                    pool.tensor_copy(out, src[HD * hh:HD * hh + HD, NPT:T].rearrange("p (b q) -> p b q", q=Q_DEC)).then_inc(sem_out, 1)

            pool.wait_ge(zeroed, 4)
            for m in range(NPAIR):
                await_query(pool, m)
                spread(qf[:, m % 2, :], m, qx_done)

            for c in range(3):
                for j in range(2):
                    await_read(pool, ("ko", c, j))
            pool.dma_start(halves(O["new_k_prompt"]), knat[:, 0:2, :]).then_inc(keys_stored, 16)
            pool.dma_start(O["new_k_sample"], knat[0:NS, 2, :]).then_inc(keys_stored, 16)
            for i in range(4):
                for c in range(2):
                    await_read(pool, ("v", i, c))
            await_read(pool, ("vs",))
            pool.dma_start(halves(O["new_v_prompt"]), V[:, 0:2, :]).then_inc(values_stored, 16)
            pool.dma_start(O["new_v_sample"], V[0:NS, 2, :]).then_inc(values_stored, 16)
            for i in range(4):
                for c in range(2):
                    await_read(pool, ("mv", i, c))
            pool.dma_start(halves(O["mem_v_prompt"]), mvN).then_inc(stored, 16)

            await_fill(pool, ("o", PAIR_ORDER[-1]))
            await_fill(pool, ("o", PAIR_ORDER[-2]))
            for g in range(2):
                for a, b in ((32, 64), (64, 128)):
                    clear(ptq[g][a:b, 2, :])

            pool.wait_ge(s_scored, 4)
            clear(qx)
            pool.dma_start(w_router, A["w_router"][0].rearrange("(k p) n -> p k n", p=P)).then_inc(late_in, 16)
            pool.dma_start(b_router, A["b_router"].rearrange("a e -> e a")).then_inc(late_in, 16)
            pool.wait_ge(zeroed, 9)
            for m in range(KB):
                await_read(pool, ("mq", m))
            for m in range(KB):
                h = m // 2
                out = qx[:, :, 4 * h:4 * h + 4].rearrange("p (b g) q -> p b g q", b=NB_DEC)[:, :, m, :]
                last = pool.tensor_copy(out, mqT[:, m, NPT:T].rearrange("p (b q) -> p b q", q=Q_DEC))
            last.then_inc(mqx_done, 1)
            await_fill(pool, ("mst", 1))
            for h in range(4):
                await_read(pool, ("mp", h))
            for part in range(3):
                pool.dma_start(bgu_f[32 * part:32 * part + 32, :], A["b_gu"][0]).then_inc(bias_in, 16)
            for c in range(2):
                for j in range(2):
                    await_read(pool, ("mko", c, j))
            pool.dma_start(halves(O["mem_k_prompt"]), mknat).then_inc(stored, 16)
            for quad in range(2):
                for f in range(2):
                    await_read(pool, ("mso", quad, f))
            for h in range(4):
                await_read(pool, ("mo", h))
            pool.wait_ge(stored, 16 * 2)
            clear(y_s)
            for h in range(2):
                pool.dma_start(y_s[64 * h:64 * h + NE, :], A["b_down"][0][:, 512 * h:512 * h + 512]).then_inc(late_in, 16)
            for i in range(2):
                clear(selT[i])
            clear(topf, -1.0)
            clear(gk)
            pool.tensor_copy(tri16, C("tri")).then_inc(zeroed, 1)
            pool.tensor_copy(one16, C("one")).then_inc(zeroed, 1)
            cleared[0] += 2
            pool.wait_ge(zeroed, cleared[0])
            for i in range(3):
                step(pool.tensor_copy(ebias_src[32 * i:32 * i + 32, :], C("eye3", 0, 32)[32 * i:32 * i + 32, :]))
                settle()
            await_fill(pool, ("var", 1))
            for a, b in ((32, 64), (64, 128)):
                clear(tokn[a:b, :, 2, :])
            pool.sem_inc(moe_ready, 1)

            for i in range(3):
                await_read(pool, ("tok", *divmod(i, 2)))
                pool.wait_ge(token_mid, i + 1)
                third_part(pool, i).then_inc(tokens_ready, 1)

            pool.wait_ge(route_ready, 2)
            blocks_done = pool.alloc_register("pool_blocks")
            pool.reg_mov(blocks_done, 0)
            base = done[0]

            def expert_block(e, first_slot):
                n = pool.snap(blocks_done)
                pool.wait_ge(picked, n + 1)
                pool.wait_ge(pool_step, n * 10 + base)
                pool.wait_ge(route_ready, 2)
                pool.tensor_copy(rcol, rankm[:, :, bass.ds(e, 1)].rearrange("p c a -> p (c a)")).then_inc(pool_step, 1)
                if first_slot is None:
                    pool.tensor_copy(slots_now, C("slot2")).then_inc(pool_step, 1)
                else:
                    pool.tensor_copy(slots_now.rearrange("p (a b) -> p a b", a=2),
                                     C("iota")[:, bass.ds(first_slot, CAP)].rearrange("p (a b) -> p a b", a=1).broadcast_to([P, 2, CAP])).then_inc(pool_step, 1)
                pool.wait_ge(pool_step, n * 10 + base + 2)
                pool.sem_inc(tables_in, 1)
                for c in range(3):
                    pool.tensor_scalar(pick[:, c, :], slots_now[:, 0:CAP], rcol[:, c:c + 1], None, ALU.is_equal).then_inc(pool_step, 1)
                pool.wait_ge(pool_step, n * 10 + base + 5)
                pool.sem_inc(sel_ready, 1)
                pool.wait_ge(sel_turned, n + 1)
                pool.wait_ge(gates_ready, 1)
                pool.tensor_copy(gcol, gates[:, :, bass.ds(e, 1)].rearrange("p c a -> p (c a)")).then_inc(pool_step, 1)
                pool.tensor_copy(ebias[0:96, :], ebias_src[0:96, bass.ds(e, 1)].broadcast_to([96, CAP])).then_inc(pool_step, 1)
                for c in range(3):
                    if c == 0:
                        pool.wait_ge(pool_step, n * 10 + base + 7)
                        pool.sem_inc(tables_in, 1)
                    pool.tensor_scalar(gpick[:, c, :], slots_now, rcol[:, c:c + 1], gcol[:, c:c + 1], ALU.is_equal, ALU.mult).then_inc(pool_step, 1)
                pool.wait_ge(pool_step, n * 10 + base + 10)
                pool.sem_inc(gates_picked, 1)
                pool.reg_add(blocks_done, blocks_done, 1)

            def expert(e, counts, at):
                more = pool.value_load(counts[0:1, bass.ds(at, 1)], min_val=0, max_val=4)
                with pool.If(more > 0):
                    with pool.Fori(0, more) as i:
                        expert_block(e, i * CAP + CAP)
                expert_block(e, None)

            with pool.Fori(0, GROUP) as e:
                expert(e, nextra, e)
            pool.wait_ge(order_ready, 1)
            with pool.Fori(GROUP, NE) as at:
                expert(pool.value_load(order[0:1, bass.ds(at, 1)], min_val=0, max_val=NE - 1), nextra_at, at)

            pool.wait_ge(ln3_in, 32)
            pool.wait_ge(fin_norm, 1)
            pool.tensor_tensor(acc[:, 0, :], acc[:, 0, :], ln3[:, 0, :], ALU.mult).then_inc(fin_pool, 1)
            pool.wait_ge(fin_pool, 1)
            pool.tensor_tensor(acc[:, 0, :], acc[:, 0, :], ln3[:, 1, :], ALU.add).then_inc(fin_pool, 1)
            pool.wait_ge(fin_norm, 2)
            pool.tensor_tensor(acc[:, 1, 512:D], acc[:, 1, 512:D], ln3[:, 0, 512:D], ALU.mult).then_inc(fin_pool, 1)
            pool.wait_ge(fin_pool, 3)
            pool.tensor_tensor(acc[:, 1, 512:D], acc[:, 1, 512:D], ln3[:, 1, 512:D], ALU.add).then_inc(fin_pool, 1)
            pool.wait_ge(keys_stored, 16 * 2)
            pool.wait_ge(values_stored, 16 * 2)
            pool.wait_ge(stored, 16 * 2)

        @block.scalar
        def _(act):
            done, exps, sticks = [0], [0], [0]

            def step(ins):
                done[0] += 1
                ins.then_inc(act_step, 1)

            def settle():
                act.wait_ge(act_step, done[0])

            def copy(out, in_, scale=1.0):
                return act.activation(out, in_, ACT.Copy, scale=scale)

            def load_table(function):
                act.wait_ge(eps_ready, 3)
                settle()
                step(act.activation(eps_small[:, 2:3], eps_small[:, 0:1], function))

            def carry(name, out, view):
                copy(out, view(await_fill(act, name))).then_inc(read_sem(name), 1)

            def wide(n):
                return lambda ps: ps[:, 0:n]

            def by(count, n, rows=P):
                return lambda ps: ps[0:rows, 0:count * n].rearrange("p (a b) -> p a b", b=n)

            carry(("x", 0, 1), xT[:, 4:8, 0:128], by(4, P))
            carry(("x", 1, 1), xT[:, 4:8, 128:256], by(4, P))

            act.wait_ge(zeroed, 4)
            for kind in "kq":
                for m in range(NPAIR):
                    if m < 4:
                        if m >= 2:
                            await_read(act, (kind + "r", m - 2))
                        elif kind == "q":
                            await_read(act, ("kr", m + 2))
                        carry((kind, m), raw[:, m % 2, :], wide(T))
                    elif kind == "k":
                        carry((kind, m), kT[:, m, :], wide(T))
                    if kind == "q" and m >= 1:
                        place_query(act, copy, m - 1)
            place_query(act, copy, NPAIR - 1)
            act.wait_ge(roped, 4)
            for m in range(4, NPAIR):
                await_read(act, ("k", m))
            for i in range(2):
                copy(ktb[i][:, :, PAST:T], kT[:, :, NPT:T]).then_inc(new_keys, 1)
            for c, (a, r) in enumerate(CHUNKS):
                carry(("ko", c, 1), knat[0:r, c, 512:D], lambda ps: ps[0:r, :])

            def values_in(items):
                for i in items:
                    carry(("v", i, 0), V[:, 0, 256 * i:256 * i + 256], wide(256))

            values_in((0, 1))

            def softmax_exp(s, p, parts, at):
                exps[0] += 1
                act.wait_ge(max_ready, exps[0])
                for i, (a, b, rows) in enumerate(parts):
                    last = act.activation(p[:, a:b], s[:, a:b], ACT.Exp, bias=small[:, at + 4 + i:at + 5 + i],
                                          accum_out=small[:, at + 8 + i:at + 9 + i])
                last.then_inc(exp_ready, 1)

            PARTS = [(0, 128, P), (384, 512, P), (128, 384, P), (512, 768, P)]

            def stick_logs(z, t, n):
                settle()
                step(act.activation(t[:, 0:n], z[:, 0:n], ACT.Abs))
                settle()
                step(act.activation(t[:, 0:n], t[:, 0:n], ACT.Exp, scale=-1.0))
                settle()
                act.activation(t[:, 0:n], t[:, 0:n], ACT.Ln, bias=1.0).then_inc(log_ready, 1)

            def prompt_stick(n):
                p = PAIR_ORDER[n]
                z = tmp[2].rearrange("p (h n) -> p h n", h=2)
                if n >= 2:
                    act.wait_ge(arg_ready, sticks[0])
                ps = await_fill(act, ("s0", p))
                copy(z[:, :, 0:P], ps[:, 0:256].rearrange("p (h n) -> p h n", h=2), ATT_SCALE).then_inc(read_sem(("s0", p)), 1)
                ps = await_fill(act, ("s1", p))
                copy(z[:, :, P:384], ps[:, :].rearrange("p (h n) -> p h n", h=2), ATT_SCALE).then_inc(read_sem(("s1", p)), 1)
                await_read(act, ("s0", p))
                await_read(act, ("s1", p))
                stick_logs(tmp[2], tmp[3], 768)

            def prompt_stick_exp(n):
                sticks[0] += 1
                act.wait_ge(arg_ready, sticks[0])
                if n >= 2:
                    await_fill(act, ("t", PAIR_ORDER[n - 2], 1))
                act.activation(tmp[6], tmp[4], ACT.Exp).then_inc(stick_ready, 1)

            def prompt_exp(n):
                if n >= 2:
                    await_fill(act, ("t", PAIR_ORDER[n - 2], 1))
                softmax_exp(tmp[0], tmp[1], PARTS, 0)

            def keys_in(kind, b):
                if kind == "ck" and b >= 2:
                    act.wait_ge(s_scored, b // 2)
                if kind == "mk":
                    act.wait_ge(s_scored, 4 + b // 2)
                for j in (1, 3):
                    carry((kind, b, j), ktb[b % 2][:, 2 * j:2 * j + 2, 0:PAST], by(2, 256))

            prompt_exp(0)
            prompt_stick(1)
            values_in((2, 3))
            ps = await_fill(act, ("vs",))
            for i in range(4):
                last = copy(V[0:NS, 2, 256 * i:256 * i + 256], ps[NS * i:NS * i + NS, 0:256])
            last.then_inc(read_sem(("vs",)), 1)
            carry(("vec",), vec[:, :], wide(40))
            act.wait_ge(keys_stored, 16 * 2)
            for c in range(2):
                carry(("m", c, 1), memT[:, 4:8, P * c:P * c + P], by(4, P))
            for n, p in enumerate(PAIR_ORDER):
                if n % 2 == 0:
                    prompt_stick_exp(n + 1)
                if n >= 2:
                    await_fill(act, ("o", PAIR_ORDER[n - 2]))
                carry(("t", p, 0), ptb[n % 2][0], wide(384))
                if n + 2 < NPAIR:
                    if n % 2 == 0:
                        prompt_exp(n + 2)
                    else:
                        prompt_stick(n + 2)
                if n % 2 == 0:
                    carry(("mv", n // 2, 0), mvN[:, 0, 128 * n:128 * n + 256], wide(256))
                else:
                    keys_in("ck", n // 2)

            def sample_stick(quad):
                act.wait_ge(s_scored, 2 * quad + 2)
                if quad == 0:
                    act.wait_ge(arg_ready, sticks[0])
                copy(tmp[2][:, 0:T], bank[5][:, 0:T], ATT_SCALE).then_inc(scores_read[1], 1)
                act.wait_ge(scores_read[1], quad + 1)
                stick_logs(tmp[2], tmp[3], T)

            def sample_stick_exp(quad):
                sticks[0] += 1
                act.wait_ge(arg_ready, sticks[0])
                if quad:
                    await_fill(act, ("st", quad - 1, 1))
                else:
                    await_fill(act, ("t", PAIR_ORDER[-1], 1))
                act.activation(tmp[6][:, 0:T], tmp[4][:, 0:T], ACT.Exp).then_inc(s_stick, 1)

            def sample_exp(quad):
                if quad:
                    await_fill(act, ("st", quad - 1, 0))
                else:
                    await_fill(act, ("t", PAIR_ORDER[-2], 1))
                softmax_exp(tmp[0], tmp[1], [(0, T, P)], 0)

            def sample_probs_in(quad):
                if quad == 0:
                    act.wait_ge(zeroed, 8)
                    await_fill(act, ("o", PAIR_ORDER[-1]))
                else:
                    act.wait_ge(s_pv, 2)
                ps = await_fill(act, ("st", quad, 0))
                copy(ptq[0][:, 0:2, :], ps[:, 0:256].rearrange("p (a b) -> p a b", b=P))
                copy(ptq[0][0:NS, 2, :], ps[0:NS, 256:384]).then_inc(read_sem(("st", quad, 0)), 1)

            def out_in(quad, f, n_pv, before):
                act.wait_ge(s_pv, n_pv)
                if before is not None:
                    await_fill(act, before)
                copy(so[0], bank[6][:, :]).then_inc(out_read[0], 1)

            sample_stick(0)
            keys_in("ck", 4)
            sample_exp(0)
            keys_in("ck", 5)
            sample_stick_exp(0)
            sample_probs_in(0)
            out_in(0, 0, 2, None)
            keys_in("ck", 6)
            keys_in("ck", 7)
            sample_stick(1)
            carry(("mk", 0), mkT[:, 0, :], wide(N_MEM))
            sample_exp(1)
            sample_stick_exp(1)
            sample_probs_in(1)
            place_sample_out(act, copy, 0, 0)
            out_in(1, 0, 4, ("so", 0, 0))
            place_sample_out(act, copy, 1, 0)

            load_table(ACT.Sqrt)
            for p in range(NPAIR):
                await_read(act, ("o", p))
            act.wait_ge(s_scored, 4)
            for g in range(2):
                for quad in range(2):
                    await_read(act, ("so", quad, g))
                act.activation(sqT[:, 4 * g:4 * g + 4, :], aT[:, 4 * g:4 * g + 4, :], ACT.Square).then_inc(sq_ready, 1)
            carry(("mk", 2), mkT[:, 2, :], wide(N_MEM))

            def root(name, eps, out):
                ps = await_fill(act, name)
                act.activation(out, ps[:, 0:T], ACT.Sqrt, bias=eps_col(eps)).then_inc(read_sem(name), 1)

            for g in range(2):
                root(("rms", g), RMS_EPS, (rstd, lnv)[g])

            def layer_norm(n, out, beta):
                load_table(ACT.Sqrt)
                for h in range(4):
                    act.wait_ge(centered, 4 * n + h + 1)
                    act.activation(sqT[:, 2 * h:2 * h + 2, :], yT[:, 2 * h:2 * h + 2, :], ACT.Square).then_inc(sq_ready, 1)
                if n == 0:
                    mid()
                    act.wait_ge(rms_done, KB)
                else:
                    act.wait_ge(norm_mul, KB)
                root(("var", n), LN_EPS, rstd)
                load_table(ACT.Exp)
                for m in range(KB):
                    act.wait_ge(norm_mul, KB * n + m + 1)
                    act.activation(out[:, m, :], yT[:, m, :], ACT.Identity, bias=vec[:, beta + m:beta + m + 1]).then_inc(norm_done, 1)

            def mid():
                carry(("mk", 4), mkT[:, 4, :], wide(N_MEM))

            layer_norm(0, x1T, 16)
            carry(("mk", 6), mkT[:, 6, :], wide(N_MEM))

            for m in range(1, KB, 2):
                carry(("mq", m), mqT[:, m, :], wide(T))

            def mem_exp(h):
                i = 2 * (h % 2)
                if h >= 2:
                    await_fill(act, ("mp", h - 2))
                softmax_exp(tmp[i], tmp[i + 1], [(0, 256, P), (256, 512, P)], 16 * (h % 2))

            def mem_probs_in(h):
                if h >= 2:
                    await_fill(act, ("mo", h - 2))
                carry(("mp", h), tmp[4 + h % 2][:, 0:512], wide(512))

            mem_exp(0)
            mem_exp(1)
            keys_in("mk", 0)
            for h in range(4):
                mem_probs_in(h)
                if h + 2 < 4:
                    mem_exp(h + 2)
            keys_in("mk", 1)

            def mem_sample_exp(quad):
                softmax_exp(tmp[6 + quad], tmp[6 + quad], [(0, 256, P)], 16 * quad)

            def mem_sample_probs_in(quad):
                act.wait_ge(s_pv, 4)
                carry(("mst", quad), ptq[quad][:, 0:2, :], by(2, P))

            keys_in("mk", 2)
            keys_in("mk", 3)
            keys_in("mk", 4)
            keys_in("mk", 5)
            mem_sample_exp(0)
            keys_in("mk", 6)
            keys_in("mk", 7)
            mem_sample_probs_in(0)
            mem_sample_exp(1)
            out_in(0, 0, 6, ("so", 1, 0))
            mem_sample_probs_in(1)
            place_mem_out(act, copy, 0, 0)
            carry(("mko", 0, 1), mknat[:, 0, 512:D], wide(512))
            out_in(1, 0, 8, ("mso", 0, 0))
            carry(("mko", 1, 1), mknat[:, 1, 512:D], wide(512))
            place_mem_out(act, copy, 1, 0)

            layer_norm(1, x2T, 32)

            act.wait_ge(late_in, 16 * LATE)
            ps = await_fill(act, ("lgT",))
            act.activation(logT[0:NE, :], ps[0:NE, 0:T], ACT.Identity, bias=b_router).then_inc(read_sem(("lgT",)), 1)

            def token_tile(i):
                c, h = divmod(i, 2)
                r = CHUNKS[c][1]
                ps = await_fill(act, ("tok", c, h))[0:r, :]
                copy(acc[:, c, 512 * h:512 * h + 512] if c < 2 else acc2[32 * h:32 * h + 32, :], ps, ALPHA)
                copy(tokn[0:r, 0, c, 512 * h:512 * h + 512], ps).then_inc(token_high, 1)

            def token_second(i):
                c, h = divmod(i, 2)
                r = CHUNKS[c][1]
                await_read(act, ("tok", c, h))
                copy(tokn[0:r, 1, c, 512 * h:512 * h + 512], token_rest[i][0:r, :]).then_inc(token_mid, 1)

            token_tile(0)
            token_tile(1)
            token_second(0)
            token_tile(2)
            token_second(1)
            token_tile(3)
            act.wait_ge(router_go, 1)
            act.wait_ge(zeroed, 14)
            for c, (a, r) in enumerate(CHUNKS):
                last = act.activation(gk[0:r, c, :], top[0:r, c, 0:TOPK], ACT.Exp, bias=small[0:r, c:c + 1],
                                      accum_out=small[0:r, 4 + c:5 + c])
            last.then_inc(router_exp, 1)
            token_tile(4)
            token_second(2)
            token_tile(5)
            for i in (3, 4, 5):
                token_second(i)
            act.sem_inc(acc_ready, 1)
            blocks_done = act.alloc_register("act_blocks")
            act.reg_mov(blocks_done, 0)

            def gathered(n):
                act.wait_ge(picked, n + 2)
                copy(xgT, bank[0][:, :].rearrange("p (a b) -> p a b", b=CAP)).then_inc(xg_ready, 1)

            gathered(0)
            act.wait_ge(zeroed, 12)
            act.wait_ge(gates_turned, 1)
            copy(selT[0][0:NE, :], bank[5][0:NE, 0:T])
            copy(selT[1][64:64 + NE, :], bank[5][0:NE, 0:T]).then_inc(selT_ready, 1)
            act.sem_inc(y_ready, 1)
            act.wait_ge(route_ready, 2)

            def expert_block(release, last_block=False):
                n = act.snap(blocks_done)
                act.wait_ge(sig_in, n + 1)
                act.activation(sig_s, gate_s, ACT.Sigmoid, scale=SW_ALPHA).then_inc(sig_ready, 1)
                act.wait_ge(act_turned, n + 1)
                copy(actT, bank[3][:, :].rearrange("p (a b) -> p a b", b=P)).then_inc(actT_ready, 1)
                act.wait_ge(sel_turned, n + 2)
                copy(selT[0][0:64, :], bank[5][0:64, 0:T])
                copy(selT[1][64:128, :], bank[5][64:128, 0:T]).then_inc(selT_ready, 1)
                if not last_block:
                    gathered(n + 1)
                act.wait_ge(down_done, n + 1)
                if release:
                    act.sem_inc(dn_used, 1)
                copy(y_s, bank[4][:, :]).then_inc(y_ready, 1)
                act.reg_add(blocks_done, blocks_done, 1)

            def further_blocks(e, counts):
                more = act.value_load(counts[0:1, bass.ds(e, 1)], min_val=0, max_val=4)
                with act.If(more > 0):
                    with act.Fori(0, more):
                        expert_block(False)

            with act.Fori(0, GROUP) as e:
                further_blocks(e, nextra)
                expert_block(True)
            act.wait_ge(order_ready, 1)
            with act.Fori(GROUP, NE - 1) as e:
                further_blocks(e, nextra_at)
                expert_block(True)
            further_blocks(NE - 1, nextra_at)
            expert_block(True, last_block=True)

            load_table(ACT.Sqrt)

            def final_root(c):
                r = CHUNKS[c][1]
                act.wait_ge(fin_var, c + 1)
                act.activation(small[0:r, 24 + c:25 + c], small[0:r, 17 + 2 * c:18 + 2 * c], ACT.Sqrt, bias=eps_col(LN_EPS, r)).then_inc(fin_root, 1)

            def final_norm(c):
                x = acc[0:CHUNKS[c][1], c, :]
                r = CHUNKS[c][1]
                act.wait_ge(fin_scale, c + 1)
                act.activation(x, x, ACT.Identity, bias=small[0:r, 28 + c:29 + c], scale=small[0:r, 24 + c:25 + c]).then_inc(fin_norm, 1)

            for c in range(3):
                final_root(c)
                final_norm(c)
            act.wait_ge(fin_ready, 2)
            act.dma_start(O["y_sample"], acc[0:NS, 2, :]).then_inc(y_stored, 16)

        @block.vector
        def _(dve):
            done, fronts, exps, logs = [0], [0], [0], [0]

            def step(ins):
                done[0] += 1
                ins.then_inc(dve_step, 1)

            def settle():
                dve.wait_ge(dve_step, done[0])

            copy = dve.tensor_copy

            def carry(name, out, view):
                copy(out, view(await_fill(dve, name))).then_inc(read_sem(name), 1)

            def wide(n):
                return lambda ps: ps[:, 0:n]

            def by(count, n, rows=P):
                return lambda ps: ps[0:rows, 0:count * n].rearrange("p (a b) -> p a b", b=n)

            dve.memset(eps_small[:, 0:1], LN_EPS).then_inc(eps_ready, 1)
            dve.memset(eps_small[:, 1:2], RMS_EPS).then_inc(eps_ready, 1)
            dve.memset(eps_small[:, 2:3], 0.0).then_inc(eps_ready, 1)
            carry(("x", 0, 0), xT[:, 0:4, 0:128], by(4, P))
            carry(("x", 1, 0), xT[:, 0:4, 128:256], by(4, P))
            carry(("x", 2, 0), xT[:, :, NPT:T], by(KB, NS))

            for kind in "kq":
                for m in range(NPAIR):
                    if m < 4:
                        await_read(dve, (kind, m))
                        if kind == "k" and m == 0:
                            dve.wait_ge(const_in, 32)
                        step(dve.tensor_tensor(rope_t[:, 0, :], raw[:, m % 2, :], C("cos"), ALU.mult))
                        ps = await_fill(dve, (kind + "r", m))
                        dve.tensor_tensor(rope_t[:, 1, :], ps[:, 0:T], C("sin"), ALU.mult).then_inc(read_sem((kind + "r", m)), 1)
                        await_read(dve, (kind + "r", m))
                        settle()
                    if kind == "k":
                        if m < 4:
                            dve.tensor_tensor(kT[:, m, :], rope_t[:, 0, :], rope_t[:, 1, :], ALU.add).then_inc(roped, 1)
                            dve.wait_ge(roped, m + 1)
                        continue
                    if m >= 2:
                        dve.wait_ge(qz_done, 2 * (m - 1))
                        dve.wait_ge(qx_done, 2 * (m - 1))
                    if m < 4:
                        dve.tensor_tensor(qf[:, m % 2, :], rope_t[:, 0, :], rope_t[:, 1, :], ALU.add).then_inc(qf_ready, 1)
                        dve.wait_ge(qf_ready, m + 1)
                    else:
                        carry((kind, m), qf[:, m % 2, :], wide(T))
            for c, (a, r) in enumerate(CHUNKS):
                carry(("ko", c, 0), knat[0:r, c, 0:512], lambda ps: ps[0:r, :])

            def values_in(items):
                for i in items:
                    carry(("v", i, 1), V[:, 1, 256 * i:256 * i + 256], wide(256))

            values_in((0, 1))

            def negate_max(s, views, at):
                settle()
                i = 0
                for v in views:
                    k = v.shape[1] if len(v.shape) == 3 else 1
                    step(dve.tensor_reduce(small[:, at + i:at + i + k], v, AX, ALU.max))
                    i += k
                settle()
                fronts[0] += 1
                dve.tensor_scalar(small[:, at + 4:at + 4 + i], small[:, at:at + i], -1.0, None, ALU.mult).then_inc(max_ready, 1)

            def divide(p, parts, at, sem_out):
                exps[0] += 1
                dve.wait_ge(exp_ready, exps[0])
                n = len(parts)
                step(dve.reciprocal(small[:, at + 12:at + 12 + n], small[:, at + 8:at + 8 + n]))
                settle()
                for i, (a, b) in enumerate(parts):
                    last = dve.tensor_scalar(p[:, a:b], p[:, a:b], small[:, at + 12 + i:at + 13 + i], None, ALU.mult)
                last.then_inc(sem_out, 1)

            def heads(t):
                return t.rearrange("p (h n) -> p h n", h=2)

            def pair_mask(name):
                return C(name).unsqueeze(1).broadcast_to([P, 2, P])

            def prompt_front(n):
                p = PAIR_ORDER[n]
                s = heads(tmp[0])
                ps = await_fill(dve, ("s0", p))[:, 0:256].rearrange("p (h n) -> p h n", h=2)
                dve.scalar_tensor_tensor(s[:, :, 0:P], ps, ATT_SCALE, pair_mask("causal"), ALU.mult, ALU.add).then_inc(read_sem(("s0", p)), 1)
                ps = heads(await_fill(dve, ("s1", p))[:, :])
                step(dve.tensor_scalar(s[:, :, P:256], ps[:, :, 0:P], ATT_SCALE, None, ALU.mult))
                dve.scalar_tensor_tensor(s[:, :, 256:384], ps[:, :, P:256], ATT_SCALE, pair_mask("causal"), ALU.mult, ALU.add).then_inc(read_sem(("s1", p)), 1)
                await_read(dve, ("s0", p))
                await_read(dve, ("s1", p))
                negate_max(tmp[0], [s[:, :, 0:P], s[:, :, P:384]], 0)

            PARTS = [(0, 128), (384, 512), (128, 384), (512, 768)]

            def suffix_sums(out, in_, ranges):
                for a, b in ranges:
                    src = in_[:, a:b][:, ::-1]
                    step(dve.tensor_tensor_scan(out[:, a:b][:, ::-1], src, C("zero").broadcast_to([P, b - a]), 0.0, ALU.add, ALU.add))

            def stick_middle(n, strict, strict_add, views, ranges):
                logs[0] += 1
                dve.wait_ge(log_ready, logs[0])
                z, l, sp, cum = tmp[2][:, 0:n], tmp[3][:, 0:n], tmp[4], tmp[5]
                step(dve.scalar_tensor_tensor(sp[:, 0:n], z, 0.0, l, ALU.max, ALU.add))
                settle()
                for v in views(sp):
                    step(dve.tensor_tensor(v, v, strict, ALU.mult))
                settle()
                suffix_sums(cum, sp, ranges)
                settle()
                step(dve.tensor_tensor(sp[:, 0:n], z, cum[:, 0:n], ALU.subtract))
                settle()
                for v in views(sp):
                    last = dve.tensor_tensor(v, v, strict_add, ALU.add)
                last.then_inc(arg_ready, 1)

            def prompt_stick(n):
                stick_middle(768, pair_mask("strict"), pair_mask("strict_add"),
                             lambda t: [heads(t)[:, :, 0:P], heads(t)[:, :, 256:384]],
                             [(0, 128), (128, 384), (384, 512), (512, 768)])

            def keys_in(kind, b):
                if kind == "ck" and b >= 2:
                    dve.wait_ge(s_scored, b // 2)
                if kind == "mk":
                    dve.wait_ge(s_scored, 4 + b // 2)
                for j in (0, 2):
                    carry((kind, b, j), ktb[b % 2][:, 2 * j:2 * j + 2, 0:PAST], by(2, 256))

            prompt_front(0)
            prompt_stick(1)
            divide(tmp[1], PARTS, 0, prob_ready)
            values_in((2, 3))
            dve.wait_ge(keys_stored, 16 * 2)
            for c in range(2):
                carry(("m", c, 0), memT[:, 0:4, P * c:P * c + P], by(4, P))
            for n, p in enumerate(PAIR_ORDER):
                if n >= 2:
                    await_fill(dve, ("o", PAIR_ORDER[n - 2]))
                carry(("t", p, 1), ptb[n % 2][1], wide(384))
                if n % 2 == 0:
                    if n + 2 < NPAIR:
                        prompt_front(n + 2)
                    carry(("o", p), aT[:, p, 0:NPT], wide(NPT))
                    carry(("mv", n // 2, 1), mvN[:, 1, 256 * (n // 2):256 * (n // 2) + 256], wide(256))
                else:
                    if n + 2 < NPAIR:
                        divide(tmp[1], PARTS, 0, prob_ready)
                    keys_in("ck", n // 2)
                    carry(("o", p), aT[:, p, 0:NPT], wide(NPT))
                    if n + 2 < NPAIR:
                        prompt_stick(n + 2)

            def sample_front(quad):
                dve.wait_ge(s_scored, 2 * quad + 2)
                s = tmp[0]
                step(dve.tensor_scalar(s[:, 0:PAST], bank[4][:, 0:PAST], ATT_SCALE, None, ALU.mult))
                dve.scalar_tensor_tensor(s[:, PAST:T], bank[4][:, PAST:T], ATT_SCALE, C("new_causal", NS * quad, NS * quad + NS),
                                         ALU.mult, ALU.add).then_inc(scores_read[0], 1)
                dve.wait_ge(scores_read[0], quad + 1)
                negate_max(s, [s[:, 0:T]], 0)

            def sample_stick(quad):
                a, b = NS * quad, NS * quad + NS
                stick_middle(T, C("new_strict", a, b), C("new_strict_add", a, b), lambda t: [t[:, PAST:T]], [(0, T)])

            def sample_probs_in(quad):
                if quad == 0:
                    dve.wait_ge(zeroed, 8)
                    await_fill(dve, ("o", PAIR_ORDER[-1]))
                else:
                    dve.wait_ge(s_pv, 2)
                ps = await_fill(dve, ("st", quad, 1))
                copy(ptq[1][:, 0:2, :], ps[:, 0:256].rearrange("p (a b) -> p a b", b=P))
                copy(ptq[1][0:NS, 2, :], ps[0:NS, 256:384]).then_inc(read_sem(("st", quad, 1)), 1)

            def out_in(quad, f, n_pv, before):
                dve.wait_ge(s_pv, n_pv)
                if before is not None:
                    await_fill(dve, before)
                copy(so[1], bank[7][:, :]).then_inc(out_read[1], 1)

            sample_front(0)
            keys_in("ck", 4)
            sample_stick(0)
            keys_in("ck", 5)
            divide(tmp[1], [(0, T)], 0, s_prob)
            sample_probs_in(0)
            out_in(0, 1, 2, None)
            keys_in("ck", 6)
            keys_in("ck", 7)
            sample_front(1)
            sample_stick(1)
            divide(tmp[1], [(0, T)], 0, s_prob)
            carry(("mk", 1), mkT[:, 1, :], wide(N_MEM))
            sample_probs_in(1)
            place_sample_out(dve, copy, 0, 1)
            out_in(1, 1, 4, ("so", 0, 1))
            place_sample_out(dve, copy, 1, 1)

            for g in range(2):
                r = (rstd, lnv)[g]
                await_read(dve, ("rms", g))
                step(dve.reciprocal(r, r))
                settle()
                if g == 0:
                    for quad in range(2):
                        await_read(dve, ("so", quad, 0))
                for m in range(4 * g, 4 * g + 4):
                    dve.scalar_tensor_tensor(aT[:, m, :], aT[:, m, :], vec[:, m:m + 1], r, ALU.mult, ALU.mult).then_inc(rms_done, 1)

            def add_residual(kind, n, x):
                for m in range(KB):
                    ps = await_fill(dve, (kind, m))
                    dve.scalar_tensor_tensor(yT[:, m, :], x[:, m, :], ALPHA, ps[:, 0:T], ALU.mult, ALU.add).then_inc(read_sem((kind, m)), 1)

            def layer_norm(n, gamma, mid):
                ps = await_fill(dve, ("mean", n))[:, 0:T].unsqueeze(1).broadcast_to([P, 2, T])
                for h in range(4):
                    y = yT[:, 2 * h:2 * h + 2, :]
                    last = dve.tensor_tensor(y, y, ps, ALU.subtract)
                    if h < 3:
                        last.then_inc(centered, 1)
                    else:
                        last.then_inc(read_sem(("mean", n)), 1)
                await_read(dve, ("mean", n))
                dve.sem_inc(centered, 1)
                if mid:
                    mid()
                await_read(dve, ("var", n))
                step(dve.reciprocal(rstd, rstd))
                settle()
                dve.wait_ge(sq_ready, 2 + 4 * n + 4)
                for m in range(KB):
                    dve.scalar_tensor_tensor(yT[:, m, :], yT[:, m, :], vec[:, gamma + m:gamma + m + 1], rstd, ALU.mult, ALU.mult).then_inc(norm_mul, 1)

            for g in range(2):
                for h in range(2):
                    await_fill(dve, ("st", 1, g))
            dve.wait_ge(s_pv, 4)
            dve.wait_ge(values_stored, 16 * 2)
            carry(("mk", 3), mkT[:, 3, :], wide(N_MEM))
            add_residual("y1", 0, xT)

            def mid():
                carry(("mk", 5), mkT[:, 5, :], wide(N_MEM))

            layer_norm(0, 8, mid)
            carry(("mk", 7), mkT[:, 7, :], wide(N_MEM))

            for m in range(0, KB, 2):
                carry(("mq", m), mqT[:, m, :], wide(T))

            def mem_front(h):
                s = tmp[2 * (h % 2)][:, 0:512]
                ps = await_fill(dve, ("ms", h))
                dve.tensor_scalar(s, ps[:, :], MEM_SCALE, None, ALU.mult).then_inc(read_sem(("ms", h)), 1)
                await_read(dve, ("ms", h))
                negate_max(s, [heads(s)], 16 * (h % 2))

            def mem_divide(h):
                divide(tmp[2 * (h % 2) + 1], [(0, 256), (256, 512)], 16 * (h % 2), prob_ready)

            mem_front(0)
            mem_front(1)
            mem_divide(0)
            keys_in("mk", 0)
            for h in range(4):
                if h + 1 < 4:
                    mem_divide(h + 1)
                if h + 2 < 4:
                    mem_front(h + 2)
                carry(("mo", h), oT[:, 2 * h:2 * h + 2, 0:NPT], by(2, 256))
            keys_in("mk", 1)

            def mem_sample_front(quad):
                dve.wait_ge(s_scored, 4 + 2 * quad + 2)
                s = tmp[6 + quad][:, 0:256]
                dve.tensor_scalar(s, bank[4 + quad][:, 0:256], MEM_SCALE, None, ALU.mult).then_inc(scores_read[0], 1)
                dve.wait_ge(scores_read[0], 2 + quad + 1)
                negate_max(s, [s], 16 * quad)

            keys_in("mk", 2)
            keys_in("mk", 3)
            keys_in("mk", 4)
            keys_in("mk", 5)
            mem_sample_front(0)
            keys_in("mk", 6)
            divide(tmp[6], [(0, 256)], 0, s_prob)
            keys_in("mk", 7)
            mem_sample_front(1)
            divide(tmp[7], [(0, 256)], 16, s_prob)
            out_in(0, 1, 6, ("so", 1, 1))
            place_mem_out(dve, copy, 0, 1)
            carry(("mko", 0, 0), mknat[:, 0, 0:512], wide(512))
            out_in(1, 1, 8, ("mso", 0, 1))
            carry(("mko", 1, 0), mknat[:, 1, 0:512], wide(512))
            place_mem_out(dve, copy, 1, 1)

            dve.wait_ge(bias_in, 16 * 3)
            step(copy(bgu[:, :], bgu_f[:, :]))
            settle()
            step(dve.tensor_tensor(bgu_r[:, :], bgu_f[:, :], bgu[:, :], ALU.subtract))
            settle()
            for a in (32, 64):
                step(copy(bgu[a:a + 32, :], bgu_r[a:a + 32, :]))
            settle()
            step(dve.tensor_tensor(bgu_r[64:96, :], bgu_r[64:96, :], bgu[64:96, :], ALU.subtract))
            settle()
            copy(bgu[64:96, :], bgu_r[64:96, :]).then_inc(bias_split, 1)
            add_residual("y2", 1, x1T)

            layer_norm(1, 24, None)

            def token_remainder(i):
                c, h = divmod(i, 2)
                r = CHUNKS[c][1]
                dve.wait_ge(token_high, i + 1)
                ps = await_fill(dve, ("tok", c, h))[0:r, :]
                dve.tensor_tensor(token_rest[i][0:r, :], ps, tokn[0:r, 0, c, 512 * h:512 * h + 512],
                                  ALU.subtract).then_inc(read_sem(("tok", c, h)), 1)

            def token_third(i):
                c, h = divmod(i, 2)
                await_read(dve, ("tok", c, h))
                dve.wait_ge(token_mid, i + 1)
                return third_part(dve, i)

            token_remainder(0)
            token_remainder(1)
            ps = await_fill(dve, ("lg",))
            step(copy(logit[:, 0:2, :], ps[:, 0:64].rearrange("p (a b) -> p a b", b=NE)))
            copy(logit[0:NS, 2, :], ps[0:NS, 64:96]).then_inc(read_sem(("lg",)), 1)
            await_read(dve, ("lg",))
            settle()
            for c, (a, r) in enumerate(CHUNKS):
                step(dve.max(top[0:r, c, :], logit[0:r, c, :]))
            settle()
            for c, (a, r) in enumerate(CHUNKS):
                last = dve.tensor_scalar(small[0:r, c:c + 1], top[0:r, c, 0:1], -1.0, None, ALU.mult)
            last.then_inc(router_go, 1)
            for c, (a, r) in enumerate(CHUNKS):
                step(dve.max_index(topi[0:r, c, :], top[0:r, c, :], logit[0:r, c, :]))
            settle()
            dve.wait_ge(zeroed, 14)
            step(copy(topf[:, 0:2, :], topi[:, 0:2, :]))
            step(copy(topf[0:NS, 2, :], topi[0:NS, 2, :]))
            settle()
            experts = C("iota", 0, NE).unsqueeze(1).broadcast_to([P, TOPK, NE])
            for c in range(3):
                step(dve.tensor_tensor(eq[:, c], experts, topf[:, c, 0:TOPK].unsqueeze(2).broadcast_to([P, TOPK, NE]), ALU.is_equal))
            settle()
            step(dve.tensor_reduce(mask, eq.rearrange("p c k e -> p c e k"), AX, ALU.add))
            settle()
            dve.tensor_copy(mask16, mask).then_inc(route_ready, 1)
            token_remainder(2)
            ps = await_fill(dve, ("rank",))
            step(dve.scalar_tensor_tensor(rankm, ps[:, 0:96].rearrange("p (a b) -> p a b", b=NE), 1.0, mask, ALU.add, ALU.mult))
            step(dve.tensor_scalar(nxf, ps[:, 96:128], float(CAP), None, ALU.is_gt))
            for k in range(2, 5):
                settle()
                if k < 4:
                    step(dve.scalar_tensor_tensor(nxf, ps[:, 96:128], float(CAP * k), nxf, ALU.is_gt, ALU.add))
                else:
                    dve.scalar_tensor_tensor(nxf, ps[:, 96:128], float(CAP * k), nxf, ALU.is_gt, ALU.add).then_inc(read_sem(("rank",)), 1)
            await_read(dve, ("rank",))
            step(dve.tensor_scalar(rankm, rankm, -1.0, None, ALU.add))
            step(copy(nextra, nxf))
            settle()
            dve.sem_inc(route_ready, 1)
            token_remainder(3)
            token_remainder(4)
            token_remainder(5)
            for i in range(3, 6):
                last = token_third(i)
            last.then_inc(tokens_ready, 1)
            dve.wait_ge(router_exp, 1)
            step(dve.reciprocal(small[:, 8:10], small[:, 4:6]))
            step(dve.reciprocal(small[0:NS, 10:11], small[0:NS, 6:7]))
            settle()
            for c, (a, r) in enumerate(CHUNKS):
                step(dve.tensor_scalar(gk[0:r, c, :], gk[0:r, c, :], small[0:r, 8 + c:9 + c], None, ALU.mult))
            settle()
            for c in range(3):
                step(dve.tensor_tensor(eqg[:, c], eq[:, c], gk[:, c, :].unsqueeze(2).broadcast_to([P, TOPK, NE]), ALU.mult))
            settle()
            dve.tensor_reduce(gates, eqg.rearrange("p c k e -> p c e k"), AX, ALU.add).then_inc(gates_ready, 1)

            ids = C("iota", GROUP, NE, 1)
            counts = nxf[0:1, GROUP:NE]
            step(dve.tensor_scalar(key, ids, -1.0, 64.0, ALU.mult, ALU.add))
            settle()
            step(dve.scalar_tensor_tensor(key, counts, 64.0, key, ALU.mult, ALU.add))
            settle()

            def across(v):
                return v.unsqueeze(1).broadcast_to([1, REST, REST])

            def down(v):
                return v.unsqueeze(2).broadcast_to([1, REST, REST])

            step(dve.tensor_tensor(cmp_s, across(key), down(key), ALU.is_gt))
            settle()
            step(dve.tensor_reduce(place, cmp_s, AX, ALU.add))
            settle()
            step(dve.tensor_tensor(cmp_s, across(place), down(C("seat", 0, REST, 1)), ALU.is_equal))
            settle()
            dve.wait_ge(tokens_ready, 4)
            for out, v in ((order, ids), (nextra_at, counts)):
                step(dve.tensor_tensor(who_s, cmp_s, across(v), ALU.mult))
                settle()
                step(dve.tensor_reduce(val, who_s, AX, ALU.add))
                settle()
                step(copy(out[0:1, GROUP:NE], val))
            settle()
            dve.sem_inc(order_ready, 1)

            dve.wait_ge(acc_ready, 1)
            dve.sem_inc(added, 1)
            blocks_done = dve.alloc_register("dve_blocks")
            dve.reg_mov(blocks_done, 0)
            COMB_BANK = (5, 0, 4, 6, 7)

            def add_output(i):
                c, h = divmod(i, 2)
                a = acc[:, c, 512 * h:512 * h + 512] if i < 4 else acc2
                ps = bank[COMB_BANK[i]][0:P if i < 4 else 64, :]
                dve.tensor_tensor(a, a, ps, ALU.add).then_inc(added, 1)

            def add_outputs(n):
                dve.wait_ge(added, n * 5 + 1)
                for i in range(5):
                    dve.wait_ge(comb, n * 5 + i + 1)
                    add_output(i)

            def expert_block(release):
                n = dve.snap(blocks_done)
                dve.wait_ge(gu_done, n + 1)
                if release:
                    dve.sem_inc(gu_used, 1)
                dve.tensor_scalar(gate_s, bank[1][:, :], LIMIT, None, ALU.min).then_inc(sig_in, 1)
                dve.tensor_scalar(up_s, bank[2][:, :], LIMIT, -LIMIT, ALU.min, ALU.max).then_inc(moe_dve, 1)
                dve.wait_ge(moe_dve, n * 2 + 1)
                dve.wait_ge(sig_in, n + 1)
                dve.scalar_tensor_tensor(up_s, up_s, 1.0, gate_s, ALU.add, ALU.mult).then_inc(moe_dve, 1)
                dve.wait_ge(moe_dve, n * 2 + 2)
                dve.wait_ge(sig_ready, n + 1)
                dve.tensor_tensor(act_s, up_s, sig_s, ALU.mult).then_inc(act_ready, 1)
                add_outputs(n)
                dve.reg_add(blocks_done, blocks_done, 1)

            def expert(e, counts):
                more = dve.value_load(counts[0:1, bass.ds(e, 1)], min_val=0, max_val=4)
                with dve.If(more > 0):
                    with dve.Fori(0, more):
                        expert_block(False)
                expert_block(True)

            with dve.Fori(0, GROUP) as e:
                expert(e, nextra)
            with dve.Fori(GROUP, NE) as e:
                expert(e, nextra_at)
            n = dve.snap(blocks_done)

            def final_add(i):
                dve.wait_ge(comb, n * 5 + i + 1)
                add_output(i)

            def final_stats(c):
                r = CHUNKS[c][1]
                st = (gate_s, sig_s, up_s)[c][0:r, 0:12]
                for h in range(2):
                    step(dve.bn_stats(st[:, 6 * h:6 * h + 6], acc[0:r, c, 512 * h:512 * h + 512]))
                settle()
                dve.bn_aggr(small[0:r, 16 + 2 * c:18 + 2 * c], st).then_inc(fin_var, 1)

            def final_scale(c):
                r = CHUNKS[c][1]
                dve.wait_ge(fin_root, c + 1)
                step(dve.reciprocal(small[0:r, 24 + c:25 + c], small[0:r, 24 + c:25 + c]))
                settle()
                dve.scalar_tensor_tensor(small[0:r, 28 + c:29 + c], small[0:r, 16 + 2 * c:17 + 2 * c], -1.0,
                                         small[0:r, 24 + c:25 + c], ALU.mult, ALU.mult).then_inc(fin_scale, 1)

            dve.wait_ge(added, n * 5 + 1)
            final_add(0)
            final_add(1)
            dve.wait_ge(added, n * 5 + 3)
            final_stats(0)
            final_add(2)
            final_add(3)
            final_scale(0)
            dve.wait_ge(added, n * 5 + 5)
            final_stats(1)
            final_add(4)
            dve.wait_ge(added, n * 5 + 6)
            for h in range(2):
                step(copy(acc[0:NS, 2, 512 * h:512 * h + 512], acc2[32 * h:32 * h + 32, :]))
            final_scale(1)
            settle()
            final_stats(2)
            final_scale(2)
            dve.wait_ge(ln3_in, 32)
            for c, n_cols in ((1, 512), (2, D)):
                r = CHUNKS[c][1]
                x = acc[0:r, c, 0:n_cols]
                dve.wait_ge(fin_norm, c + 1)
                step(dve.tensor_tensor(x, x, ln3[0:r, 0, 0:n_cols], ALU.mult))
                settle()
                dve.tensor_tensor(x, x, ln3[0:r, 1, 0:n_cols], ALU.add).then_inc(fin_ready, 1)


_INS = ["x_prompt", "x_sample", "mem_prompt", "cache_k", "cache_v", "cache_mem_k", "cache_mem_v", "page_table",
        "w_in", "g_moba", "g_sb", "w_out", "ln1_g", "ln1_b", "w_mq", "w_mkv", "w_mo", "ln2_g", "ln2_b",
        "w_router", "b_router", "w_gu", "b_gu", "w_down", "b_down", "ln3_g", "ln3_b"]
_OUTS = [("y_prompt", (256, 1024), (1, 256, 1024)), ("y_sample", (32, 1024), (8, 4, 1024)),
         ("new_k_prompt", (256, 1024), (1, 1, 256, 16, 64)), ("new_v_prompt", (256, 1024), (1, 1, 256, 16, 64)),
         ("new_k_sample", (32, 1024), (1, 8, 4, 16, 64)), ("new_v_sample", (32, 1024), (1, 8, 4, 16, 64)),
         ("mem_k_prompt", (256, 1024), (1, 1, 256, 4, 256)), ("mem_v_prompt", (256, 1024), (1, 1, 256, 4, 256))]


def kernel(**inputs):
    import numpy as _np
    import concourse.bacc as _bacc
    from concourse.bass_utils import run_bass_kernel_spmd as _run

    nc = _bacc.Bacc("TRN2", target_bir_lowering=False, num_devices=1)
    arrays, ins, outs = {}, {}, {}
    for name in _INS:
        a = _np.ascontiguousarray(inputs[name])
        arrays[f"in_{name}"] = a
        ins[name] = nc.dram_tensor(f"in_{name}", a.shape, mybir.dt.from_np(a.dtype), kind="ExternalInput").ap()
    c = const_table()
    arrays["in_consts"] = c
    ins["consts"] = nc.dram_tensor("in_consts", c.shape, F32, kind="ExternalInput").ap()
    for name, shape, _ in _OUTS:
        outs[name] = nc.dram_tensor(f"out_{name}", shape, F32, kind="ExternalOutput").ap()
    build(nc, ins, outs)
    r = _run(nc, [arrays], core_ids=[0])
    return tuple(r.results[0][f"out_{name}"].reshape(shape) for name, _, shape in _OUTS)
```
